# Optimizing a Trainium2 kernel written in Bass

```python
import math
import jax, jax.numpy as jnp
from jax import lax
import numpy as np

D_MODEL = 1024
BATCH = 1
SEQ = 256
DEPTH = 2

GRID_W = 64
CTX_LEN = 256
CONV_WIDTH = 512
CONV_K = 31
N_HEADS = 8
QK_DIM = 64
V_DIM = 2 * QK_DIM
ATTN_WIDTH = N_HEADS * V_DIM
QK_COLS = N_HEADS * 2 * QK_DIM
D_FF = 4 * D_MODEL
ROPE_BASE = 10000.0
N_FREQ_AXIS = QK_DIM // 4
Q_BLOCK = 128
EPS = 1e-6

CONV_OFF = 0
Q_OFF = CONV_OFF + 2 * CONV_WIDTH
K_OFF = Q_OFF + QK_COLS
V_OFF = K_OFF + QK_COLS
GATE_OFF = V_OFF + ATTN_WIDTH
IN_COLS = GATE_OFF + 2 * D_MODEL


def rmsnorm(x, g):
    xf = x.astype(jnp.float32)
    y = xf * lax.rsqrt(jnp.mean(xf * xf, axis=-1, keepdims=True) + EPS)
    return (y * g.astype(jnp.float32)).astype(x.dtype)

def layernorm(x, g, b):
    xf = x.astype(jnp.float32)
    mu = jnp.mean(xf, axis=-1, keepdims=True)
    var = jnp.mean(jnp.square(xf - mu), axis=-1, keepdims=True)
    y = (xf - mu) * lax.rsqrt(var + EPS)
    return (y * g.astype(jnp.float32) + b.astype(jnp.float32)).astype(x.dtype)

def modulate(h, shift, scale):
    return h * (1 + scale) + shift

def axial_rope(n_tokens):
    rows = n_tokens // GRID_W
    row = jnp.repeat(jnp.arange(rows, dtype=jnp.float32), GRID_W)
    col = jnp.tile(jnp.arange(GRID_W, dtype=jnp.float32), rows)
    inv = jnp.power(ROPE_BASE, -jnp.arange(N_FREQ_AXIS, dtype=jnp.float32) / N_FREQ_AXIS)
    ang = jnp.concatenate([row[:, None] * inv, col[:, None] * inv], axis=-1)
    return jnp.cos(ang)[:, None, None, :], jnp.sin(ang)[:, None, None, :]

def apply_rope(t, cos, sin):
    cos = cos.astype(t.dtype)
    sin = sin.astype(t.dtype)
    half = QK_DIM // 2
    t1, t2 = t[..., :half], t[..., half:]
    return jnp.concatenate([t1 * cos - t2 * sin, t2 * cos + t1 * sin], axis=-1)

def diff_attention(q, keys, vals, lam, sub_g, lam_init):
    B, L = q.shape[:2]
    nb = L // Q_BLOCK
    scale = QK_DIM ** -0.5
    qb = q.reshape(B, nb, Q_BLOCK, N_HEADS, 2, QK_DIM).transpose(1, 0, 2, 3, 4, 5)

    def block(qi):
        s = jnp.einsum('bqhcd,bkhcd->bhcqk', qi, keys,
                       preferred_element_type=jnp.float32) * scale
        p = jax.nn.softmax(s, axis=-1)
        w = p[:, :, 0] - lam * p[:, :, 1]
        return jnp.einsum('bhqk,bkhv->bqhv', w.astype(vals.dtype), vals)

    out = lax.map(block, qb)
    out = out.transpose(1, 0, 2, 3, 4).reshape(B, L, N_HEADS, V_DIM)
    out = rmsnorm(out, sub_g) * (1.0 - lam_init)
    return out.reshape(B, L, ATTN_WIDTH)

def conformer_conv(u, w_dw, b_dw, ln_g, ln_b):
    a, g = u[..., :CONV_WIDTH], u[..., CONV_WIDTH:]
    z = a * jax.nn.sigmoid(g)
    pad = CONV_K // 2
    z = lax.conv_general_dilated(z, w_dw[:, None, :].astype(z.dtype), window_strides=(1,),
                                 padding=[(pad, pad)], dimension_numbers=('NWC', 'WIO', 'NWC'),
                                 feature_group_count=CONV_WIDTH) + b_dw
    return jax.nn.silu(layernorm(z, ln_g, ln_b))

def merge_branches(conv_in, attn, gate_logits, w_dw, b_dw, ln_g, ln_b,
                   w_conv_out, w_attn_out, b_gate, w_out):
    y_conv = conformer_conv(conv_in, w_dw, b_dw, ln_g, ln_b) @ w_conv_out
    y_attn = attn @ w_attn_out
    g = jax.nn.sigmoid(gate_logits + b_gate)
    g_conv, g_attn = g[..., :D_MODEL], g[..., D_MODEL:]
    return (g_conv * y_conv + g_attn * y_attn) @ w_out

def sqrelu_mlp(h, w1, w2):
    return jnp.square(jax.nn.relu(h @ w1)) @ w2

def first_inputs(seed: int = 0) -> dict:
    key = jax.random.key(seed)
    ks = jax.random.split(key, 26)
    f = jnp.float32
    nrm = lambda k, shape, s: (jax.random.normal(k, shape, f) * s).astype(f)
    return {
        "x": nrm(ks[0], (BATCH, SEQ, D_MODEL), 1.0),
        "c": nrm(ks[1], (BATCH, D_MODEL), 1.0),
        "ctx": nrm(ks[2], (BATCH, CTX_LEN, D_MODEL), 1.0),
        "c_ctx": nrm(ks[3], (D_MODEL,), 1.0),
        "w_ada": nrm(ks[4], (DEPTH, D_MODEL, 6 * D_MODEL), 0.5 * D_MODEL ** -0.5),
        "b_ada": nrm(ks[5], (DEPTH, 6 * D_MODEL), 0.02),
        "norm1_g": 1.0 + nrm(ks[6], (DEPTH, D_MODEL), 0.02),
        "w_in": nrm(ks[7], (DEPTH, D_MODEL, IN_COLS), D_MODEL ** -0.5),
        "b_gate": nrm(ks[8], (DEPTH, 2 * D_MODEL), 0.02),
        "q_norm_g": 1.0 + nrm(ks[9], (DEPTH, QK_DIM), 0.02),
        "k_norm_g": 1.0 + nrm(ks[10], (DEPTH, QK_DIM), 0.02),
        "lam_q": nrm(ks[11], (DEPTH, 2, QK_DIM), 0.1),
        "lam_k": nrm(ks[12], (DEPTH, 2, QK_DIM), 0.1),
        "attn_norm_g": 1.0 + nrm(ks[13], (DEPTH, V_DIM), 0.02),
        "w_dw": nrm(ks[14], (DEPTH, CONV_K, CONV_WIDTH), CONV_K ** -0.5),
        "b_dw": nrm(ks[15], (DEPTH, CONV_WIDTH), 0.02),
        "conv_ln_g": 1.0 + nrm(ks[16], (DEPTH, CONV_WIDTH), 0.02),
        "conv_ln_b": nrm(ks[17], (DEPTH, CONV_WIDTH), 0.02),
        "w_conv_out": nrm(ks[18], (DEPTH, CONV_WIDTH, D_MODEL), CONV_WIDTH ** -0.5),
        "w_attn_out": nrm(ks[19], (DEPTH, ATTN_WIDTH, D_MODEL), ATTN_WIDTH ** -0.5),
        "w_out": nrm(ks[20], (DEPTH, D_MODEL, D_MODEL), D_MODEL ** -0.5),
        "norm2_g": 1.0 + nrm(ks[21], (DEPTH, D_MODEL), 0.02),
        "w_mlp1": nrm(ks[22], (DEPTH, D_MODEL, D_FF), D_MODEL ** -0.5),
        "w_mlp2": nrm(ks[23], (DEPTH, D_FF, D_MODEL), D_FF ** -0.5),
    }

def first_block(x, c, ctx, c_ctx, w_ada, b_ada, norm1_g, w_in, b_gate, q_norm_g, k_norm_g,
              lam_q, lam_k, attn_norm_g, w_dw, b_dw, conv_ln_g, conv_ln_b, w_conv_out,
              w_attn_out, w_out, norm2_g, w_mlp1, w_mlp2):
    B, S, _ = x.shape
    C = ctx.shape[1]
    cos, sin = axial_rope(S)
    silu_c = jax.nn.silu(c)
    silu_cc = jax.nn.silu(c_ctx)
    h_ctx = ctx

    for i in range(DEPTH):
        last = i == DEPTH - 1
        lam_init = 0.8 - 0.6 * math.exp(-0.3 * i)
        lq = lam_q[i].astype(jnp.float32)
        lk = lam_k[i].astype(jnp.float32)
        lam = jnp.exp(jnp.sum(lq[0] * lk[0])) - jnp.exp(jnp.sum(lq[1] * lk[1])) + lam_init

        mx = (silu_c @ w_ada[i] + b_ada[i])[:, None, :]
        mc = silu_cc @ w_ada[i] + b_ada[i]
        sx1, ax1, gx1, sx2, ax2, gx2 = jnp.split(mx, 6, axis=-1)
        sc1, ac1, gc1, sc2, ac2, gc2 = jnp.split(mc, 6, axis=-1)

        hc = modulate(rmsnorm(h_ctx, norm1_g[i]), sc1, ac1)
        if last:
            kv_c = hc @ w_in[i][:, K_OFF:GATE_OFF]
            k_c, v_c = kv_c[..., :QK_COLS], kv_c[..., QK_COLS:]
        else:
            pc = hc @ w_in[i]
            conv_c = pc[..., CONV_OFF:Q_OFF]
            q_c = pc[..., Q_OFF:K_OFF]
            k_c = pc[..., K_OFF:V_OFF]
            v_c = pc[..., V_OFF:GATE_OFF]
            g_c = pc[..., GATE_OFF:]
        k_c = rmsnorm(k_c.reshape(B, C, N_HEADS, 2, QK_DIM), k_norm_g[i])
        v_c = v_c.reshape(B, C, N_HEADS, V_DIM)

        hx = modulate(rmsnorm(x, norm1_g[i]), sx1, ax1)
        px = hx @ w_in[i]
        conv_x = px[..., CONV_OFF:Q_OFF]
        q_x = px[..., Q_OFF:K_OFF].reshape(B, S, N_HEADS, 2, QK_DIM)
        k_x = px[..., K_OFF:V_OFF].reshape(B, S, N_HEADS, 2, QK_DIM)
        v_x = px[..., V_OFF:GATE_OFF].reshape(B, S, N_HEADS, V_DIM)
        g_x = px[..., GATE_OFF:]
        q_x = apply_rope(rmsnorm(q_x, q_norm_g[i]), cos, sin)
        k_x = apply_rope(rmsnorm(k_x, k_norm_g[i]), cos, sin)
        keys = jnp.concatenate([k_x, k_c], axis=1)
        vals = jnp.concatenate([v_x, v_c], axis=1)
        attn_x = diff_attention(q_x, keys, vals, lam, attn_norm_g[i], lam_init)
        y_x = merge_branches(conv_x, attn_x, g_x, w_dw[i], b_dw[i], conv_ln_g[i], conv_ln_b[i],
                             w_conv_out[i], w_attn_out[i], b_gate[i], w_out[i])
        x = x + gx1 * y_x

        if not last:
            q_c = rmsnorm(q_c.reshape(B, C, N_HEADS, 2, QK_DIM), q_norm_g[i])
            attn_c = diff_attention(q_c, k_c, v_c, lam, attn_norm_g[i], lam_init)
            y_c = merge_branches(conv_c, attn_c, g_c, w_dw[i], b_dw[i], conv_ln_g[i],
                                 conv_ln_b[i], w_conv_out[i], w_attn_out[i], b_gate[i], w_out[i])
            h_ctx = h_ctx + gc1 * y_c

        x = x + gx2 * sqrelu_mlp(modulate(rmsnorm(x, norm2_g[i]), sx2, ax2), w_mlp1[i], w_mlp2[i])
        if not last:
            h_ctx = h_ctx + gc2 * sqrelu_mlp(modulate(rmsnorm(h_ctx, norm2_g[i]), sc2, ac2),
                                             w_mlp1[i], w_mlp2[i])
    return x


A_HEAD_DIM = 64
A_Q_HEADS = 8
A_KV_HEADS = 2
WINDOW = 128
ROPE_THETA = 10000.0
B_HEADS = 4
B_HEAD_DIM = 128
B_CONV = 4
B_CHUNK = 64
LRU_WIDTH = D_MODEL
LRU_BLOCKS = 4
LRU_CONV = 4
LRU_C = 8.0
D_FF_2 = 4 * D_MODEL
A_Q_W = A_Q_HEADS * A_HEAD_DIM
A_KV_W = A_KV_HEADS * A_HEAD_DIM
B_W = B_HEADS * B_HEAD_DIM
HYB_SPLITS = (A_Q_W, A_KV_W, A_KV_W, 3 * B_W, B_W, B_HEADS, B_HEADS)
HYB_PROJ = A_Q_W + 2 * A_KV_W + 4 * B_W + 2 * B_HEADS
MIX_W = A_Q_W + B_W
N_HYB = (DEPTH + 1) // 2
N_REC = DEPTH // 2
DN_ALPHA = (2 * DEPTH) ** 0.25
DN_BETA = (8 * DEPTH) ** -0.25
LN_EPS = 1e-5
NORM_EPS = 1e-6


def split_cols(t, sizes):
    out, start = [], 0
    for s in sizes:
        out.append(t[..., start:start + s])
        start += s
    return out

def layer_norm(x, g, b):
    xf = x.astype(jnp.float32)
    mu = jnp.mean(xf, axis=-1, keepdims=True)
    var = jnp.mean(jnp.square(xf - mu), axis=-1, keepdims=True)
    y = (xf - mu) * lax.rsqrt(var + LN_EPS) * g.astype(jnp.float32) + b.astype(jnp.float32)
    return y.astype(x.dtype)

def l2_normalize(x):
    xf = x.astype(jnp.float32)
    return xf * lax.rsqrt(jnp.sum(xf * xf, axis=-1, keepdims=True) + NORM_EPS)

def apply_rope_2(x):
    T, dh = x.shape[1], x.shape[-1]
    half = dh // 2
    inv_freq = ROPE_THETA ** (-jnp.arange(half, dtype=jnp.float32) / half)
    ang = jnp.arange(T, dtype=jnp.float32)[:, None] * inv_freq[None, :]
    cos = jnp.cos(ang)[None, :, None, :]
    sin = jnp.sin(ang)[None, :, None, :]
    xf = x.astype(jnp.float32)
    x1, x2 = xf[..., :half], xf[..., half:]
    return jnp.concatenate([x1 * cos - x2 * sin, x2 * cos + x1 * sin], axis=-1).astype(x.dtype)

def causal_dwconv(x, w, b=None):
    K = w.shape[0]
    T = x.shape[1]
    xp = jnp.pad(x, ((0, 0), (K - 1, 0), (0, 0)))
    y = sum(xp[:, j:j + T] * w[j] for j in range(K))
    if b is not None:
        y = y + b
    return y

def sliding_window_attention(q, k, v, sinks):
    f32 = jnp.float32
    bsz, T, HQ, DH = q.shape
    HKV = k.shape[2]
    G = HQ // HKV
    W = WINDOW
    NB = T // W
    qb = q.reshape(bsz, NB, W, HKV, G, DH)

    def band(t):
        prev = jnp.pad(t, ((0, 0), (W, 0), (0, 0), (0, 0)))[:, :T]
        return jnp.concatenate([prev.reshape(bsz, NB, W, HKV, DH),
                                t.reshape(bsz, NB, W, HKV, DH)], axis=2)

    kb, vb = band(k), band(v)
    s = jnp.einsum('bnqhgd,bnkhd->bnhgqk', qb, kb).astype(f32) * (DH ** -0.5)
    dist = (jnp.arange(W)[:, None] + W) - jnp.arange(2 * W)[None, :]
    in_window = (dist >= 0) & (dist < W)
    key_pos = (jnp.arange(NB)[:, None] - 1) * W + jnp.arange(2 * W)[None, :]
    mask = in_window[None] & (key_pos >= 0)[:, None, :]
    s = jnp.where(mask[None, :, None, None], s, -jnp.inf)
    sink = jnp.broadcast_to(sinks.astype(f32).reshape(1, 1, HKV, G, 1, 1), s.shape[:-1] + (1,))
    p = jax.nn.softmax(jnp.concatenate([s, sink], axis=-1), axis=-1)[..., :-1]
    o = jnp.einsum('bnhgqk,bnkhd->bnqhgd', p.astype(v.dtype), vb)
    return o.reshape(bsz, T, HQ * DH)

def gated_delta_rule(q, k, v, g, beta):
    f32 = jnp.float32
    bsz, T, H, DK = q.shape
    DV = v.shape[-1]
    C = B_CHUNK
    N = T // C

    def chunk(t):
        t = t.astype(f32).reshape((bsz, N, C, H) + t.shape[3:])
        return jnp.moveaxis(t, 3, 1)

    q = chunk(q) * (DK ** -0.5)
    k = chunk(k)
    v = chunk(v)
    g = jnp.cumsum(chunk(g), axis=-1)
    beta = chunk(beta)
    k_beta = k * beta[..., None]
    v_beta = v * beta[..., None]
    idx = jnp.arange(C)
    incl = idx[:, None] >= idx[None, :]
    strict = idx[:, None] > idx[None, :]
    diff = g[..., :, None] - g[..., None, :]
    decay_incl = jnp.exp(jnp.where(incl, diff, -jnp.inf))
    decay_strict = jnp.where(strict, decay_incl, 0.0)
    a_mat = jnp.einsum('bhnik,bhnjk->bhnij', k_beta, k) * decay_strict
    eye = jnp.eye(C, dtype=f32)
    t_mat = lax.linalg.triangular_solve(a_mat + eye, jnp.broadcast_to(eye, a_mat.shape),
                                        left_side=True, lower=True, unit_diagonal=True)
    u = jnp.einsum('bhnij,bhnjv->bhniv', t_mat, v_beta)
    w = jnp.einsum('bhnij,bhnjk->bhnik', t_mat, k_beta * jnp.exp(g)[..., None])
    qk = jnp.einsum('bhnik,bhnjk->bhnij', q, k) * decay_incl
    q_g = q * jnp.exp(g)[..., None]
    g_last = g[..., -1]
    k_tail = k * jnp.exp(g_last[..., None] - g)[..., None]
    xs = tuple(jnp.moveaxis(t, 2, 0) for t in (q_g, k_tail, u, w, qk, g_last))

    def step(S, inp):
        q_c, kt_c, u_c, w_c, qk_c, gl_c = inp
        v_new = u_c - jnp.einsum('bhck,bhkv->bhcv', w_c, S)
        o_c = jnp.einsum('bhck,bhkv->bhcv', q_c, S) + jnp.einsum('bhij,bhjv->bhiv', qk_c, v_new)
        S = S * jnp.exp(gl_c)[..., None, None] + jnp.einsum('bhck,bhcv->bhkv', kt_c, v_new)
        return S, o_c

    S0 = jnp.zeros((bsz, H, DK, DV), f32)
    _, o = lax.scan(step, S0, xs)
    return jnp.transpose(o, (1, 0, 3, 2, 4)).reshape(bsz, T, H, DV)

def hybrid_mixer(x, w_in, sinks, conv_w, a_log, dt_bias, norm_w, w_out):
    f32 = jnp.float32
    bsz, T, _ = x.shape
    proj = x @ w_in
    qa, ka, va, qkv_b, z, beta_logit, a_logit = split_cols(proj, HYB_SPLITS)
    qa = apply_rope_2(qa.reshape(bsz, T, A_Q_HEADS, A_HEAD_DIM))
    ka = apply_rope_2(ka.reshape(bsz, T, A_KV_HEADS, A_HEAD_DIM))
    va = va.reshape(bsz, T, A_KV_HEADS, A_HEAD_DIM)
    o_a = sliding_window_attention(qa, ka, va, sinks)
    qkv_b = jax.nn.silu(causal_dwconv(qkv_b, conv_w))
    qb, kb, vb = split_cols(qkv_b, (B_W, B_W, B_W))
    qb = l2_normalize(qb.reshape(bsz, T, B_HEADS, B_HEAD_DIM))
    kb = l2_normalize(kb.reshape(bsz, T, B_HEADS, B_HEAD_DIM))
    vb = vb.reshape(bsz, T, B_HEADS, B_HEAD_DIM)
    beta = jax.nn.sigmoid(beta_logit.astype(f32))
    g = -jnp.exp(a_log.astype(f32)) * jax.nn.softplus(a_logit.astype(f32) + dt_bias.astype(f32))
    o_b = gated_delta_rule(qb, kb, vb, g, beta)
    o_b = o_b * lax.rsqrt(jnp.mean(o_b * o_b, axis=-1, keepdims=True) + NORM_EPS) * norm_w.astype(f32)
    o_b = o_b * jax.nn.silu(z.astype(f32).reshape(bsz, T, B_HEADS, B_HEAD_DIM))
    o_b = o_b.reshape(bsz, T, B_W).astype(x.dtype)
    return jnp.concatenate([o_a, o_b], axis=-1) @ w_out

def rg_lru(x, w_a, b_a, w_x, b_x, lam):
    f32 = jnp.float32
    bsz, T, W = x.shape
    xh = x.reshape(bsz, T, LRU_BLOCKS, W // LRU_BLOCKS)
    r = jax.nn.sigmoid((jnp.einsum('bthi,hij->bthj', xh, w_a).reshape(bsz, T, W) + b_a).astype(f32))
    i = jax.nn.sigmoid((jnp.einsum('bthi,hij->bthj', xh, w_x).reshape(bsz, T, W) + b_x).astype(f32))
    log_a = -LRU_C * r * jax.nn.softplus(-lam.astype(f32))
    a = jnp.exp(log_a)
    b = jnp.sqrt(-jnp.expm1(2.0 * log_a)) * (i * x.astype(f32))

    def combine(c1, c2):
        a1, b1 = c1
        a2, b2 = c2
        return a1 * a2, a2 * b1 + b2

    _, h = lax.associative_scan(combine, (a, b), axis=1)
    return h.astype(x.dtype)

def recurrent_mixer(x, w_in, conv_w, conv_b, w_a, b_a, w_x, b_x, lam, w_out):
    proj = x @ w_in
    xr, gate = split_cols(proj, (LRU_WIDTH, LRU_WIDTH))
    xr = causal_dwconv(xr, conv_w, conv_b)
    h = rg_lru(xr, w_a, b_a, w_x, b_x, lam)
    return (h * jax.nn.gelu(gate)) @ w_out

def sqrelu_mlp_2(x, w1, w2):
    h = jax.nn.relu(x @ w1)
    return (h * h) @ w2

def second_inputs(seed: int = 0) -> dict:
    key = jax.random.key(seed)
    ks = jax.random.split(key, 24)
    f32 = jnp.float32

    def nrm(k, shape, scale):
        return jax.random.normal(k, shape, f32) * scale

    bw = LRU_WIDTH // LRU_BLOCKS
    x = nrm(ks[0], (BATCH, SEQ, D_MODEL), 1.0)
    hyb_w_in = nrm(ks[1], (N_HYB, D_MODEL, HYB_PROJ), D_MODEL ** -0.5)
    hyb_sinks = nrm(ks[2], (N_HYB, A_Q_HEADS), 0.5)
    hyb_conv_w = nrm(ks[3], (N_HYB, B_CONV, 3 * B_W), B_CONV ** -0.5)
    hyb_a_log = jnp.log(jax.random.uniform(ks[4], (N_HYB, B_HEADS), f32, 1.0, 16.0))
    dt = jnp.exp(jax.random.uniform(ks[5], (N_HYB, B_HEADS), f32, math.log(1e-3), math.log(1e-1)))
    hyb_dt_bias = dt + jnp.log(-jnp.expm1(-dt))
    hyb_norm_w = 1.0 + nrm(ks[6], (N_HYB, B_HEAD_DIM), 0.02)
    hyb_w_out = nrm(ks[7], (N_HYB, MIX_W, D_MODEL), DN_BETA * MIX_W ** -0.5)
    rec_w_in = nrm(ks[8], (N_REC, D_MODEL, 2 * LRU_WIDTH), D_MODEL ** -0.5)
    rec_conv_w = nrm(ks[9], (N_REC, LRU_CONV, LRU_WIDTH), LRU_CONV ** -0.5)
    rec_conv_b = nrm(ks[10], (N_REC, LRU_WIDTH), 0.02)
    rec_w_a = nrm(ks[11], (N_REC, LRU_BLOCKS, bw, bw), bw ** -0.5)
    rec_b_a = nrm(ks[12], (N_REC, LRU_WIDTH), 0.02)
    rec_w_x = nrm(ks[13], (N_REC, LRU_BLOCKS, bw, bw), bw ** -0.5)
    rec_b_x = nrm(ks[14], (N_REC, LRU_WIDTH), 0.02)
    u = jax.random.uniform(ks[15], (N_REC, LRU_WIDTH), f32, 0.9, 0.999)
    a0 = u ** (1.0 / LRU_C)
    rec_lambda = jnp.log(a0) - jnp.log1p(-a0)
    rec_w_out = nrm(ks[16], (N_REC, LRU_WIDTH, D_MODEL), DN_BETA * LRU_WIDTH ** -0.5)
    ln1_g = 1.0 + nrm(ks[17], (DEPTH, D_MODEL), 0.02)
    ln1_b = nrm(ks[18], (DEPTH, D_MODEL), 0.02)
    mlp_w1 = nrm(ks[19], (DEPTH, D_MODEL, D_FF_2), D_MODEL ** -0.5)
    mlp_w2 = nrm(ks[20], (DEPTH, D_FF_2, D_MODEL), DN_BETA * D_FF_2 ** -0.5)
    ln2_g = 1.0 + nrm(ks[21], (DEPTH, D_MODEL), 0.02)
    ln2_b = nrm(ks[22], (DEPTH, D_MODEL), 0.02)
    return {'x': x, 'hyb_w_in': hyb_w_in, 'hyb_sinks': hyb_sinks, 'hyb_conv_w': hyb_conv_w,
            'hyb_a_log': hyb_a_log, 'hyb_dt_bias': hyb_dt_bias, 'hyb_norm_w': hyb_norm_w,
            'hyb_w_out': hyb_w_out, 'rec_w_in': rec_w_in, 'rec_conv_w': rec_conv_w,
            'rec_conv_b': rec_conv_b, 'rec_w_a': rec_w_a, 'rec_b_a': rec_b_a, 'rec_w_x': rec_w_x,
            'rec_b_x': rec_b_x, 'rec_lambda': rec_lambda, 'rec_w_out': rec_w_out,
            'ln1_g': ln1_g, 'ln1_b': ln1_b, 'mlp_w1': mlp_w1, 'mlp_w2': mlp_w2,
            'ln2_g': ln2_g, 'ln2_b': ln2_b}

def second_block(x, hyb_w_in, hyb_sinks, hyb_conv_w, hyb_a_log, hyb_dt_bias, hyb_norm_w, hyb_w_out,
              rec_w_in, rec_conv_w, rec_conv_b, rec_w_a, rec_b_a, rec_w_x, rec_b_x, rec_lambda,
              rec_w_out, ln1_g, ln1_b, mlp_w1, mlp_w2, ln2_g, ln2_b):
    for layer in range(DEPTH):
        j = layer // 2
        if layer % 2 == 0:
            mix = hybrid_mixer(x, hyb_w_in[j], hyb_sinks[j], hyb_conv_w[j], hyb_a_log[j],
                               hyb_dt_bias[j], hyb_norm_w[j], hyb_w_out[j])
        else:
            mix = recurrent_mixer(x, rec_w_in[j], rec_conv_w[j], rec_conv_b[j], rec_w_a[j],
                                  rec_b_a[j], rec_w_x[j], rec_b_x[j], rec_lambda[j], rec_w_out[j])
        x = layer_norm(DN_ALPHA * x + mix, ln1_g[layer], ln1_b[layer])
        x = layer_norm(DN_ALPHA * x + sqrelu_mlp_2(x, mlp_w1[layer], mlp_w2[layer]), ln2_g[layer], ln2_b[layer])
    return x


def setup_inputs(seed=0):
    out = dict(first_inputs(seed))
    for name, value in second_inputs(seed + 1).items():
        if name != "x":
            out[name + "_2"] = value
    return out


def reference(
    x, c, ctx, c_ctx, w_ada, b_ada, norm1_g, w_in, b_gate, q_norm_g, k_norm_g, lam_q, lam_k,
    attn_norm_g, w_dw, b_dw, conv_ln_g, conv_ln_b, w_conv_out, w_attn_out, w_out, norm2_g,
    w_mlp1, w_mlp2, hyb_w_in_2, hyb_sinks_2, hyb_conv_w_2, hyb_a_log_2, hyb_dt_bias_2,
    hyb_norm_w_2, hyb_w_out_2, rec_w_in_2, rec_conv_w_2, rec_conv_b_2, rec_w_a_2, rec_b_a_2,
    rec_w_x_2, rec_b_x_2, rec_lambda_2, rec_w_out_2, ln1_g_2, ln1_b_2, mlp_w1_2, mlp_w2_2,
    ln2_g_2, ln2_b_2,
):
    x = first_block(
        x, c, ctx, c_ctx, w_ada, b_ada, norm1_g, w_in, b_gate, q_norm_g, k_norm_g, lam_q, lam_k,
        attn_norm_g, w_dw, b_dw, conv_ln_g, conv_ln_b, w_conv_out, w_attn_out, w_out, norm2_g,
        w_mlp1, w_mlp2,
    )
    return second_block(
        x, hyb_w_in_2, hyb_sinks_2, hyb_conv_w_2, hyb_a_log_2, hyb_dt_bias_2, hyb_norm_w_2,
        hyb_w_out_2, rec_w_in_2, rec_conv_w_2, rec_conv_b_2, rec_w_a_2, rec_b_a_2, rec_w_x_2,
        rec_b_x_2, rec_lambda_2, rec_w_out_2, ln1_g_2, ln1_b_2, mlp_w1_2, mlp_w2_2, ln2_g_2,
        ln2_b_2,
    )


_drawn_inputs = setup_inputs


def setup_inputs(seed=0):
    import zlib

    import numpy as np

    out = dict(_drawn_inputs(seed))
    spreads = {}
    factors = {'norm1_g': 8.0,
     'b_gate': 8.0,
     'q_norm_g': 8.0,
     'k_norm_g': 8.0,
     'lam_q': 5.13,
     'lam_k': 4.202,
     'attn_norm_g': 8.0,
     'b_dw': 8.0,
     'conv_ln_g': 8.0,
     'conv_ln_b': 8.0,
     'norm2_g': 3.929,
     'hyb_sinks_2': 64.0,
     'hyb_norm_w_2': 23.746,
     'rec_conv_b_2': 3.19,
     'rec_b_a_2': 49.888,
     'rec_b_x_2': 8.0}
    for name, (base, spread) in spreads.items():
        noise = np.random.default_rng([zlib.crc32(name.encode()), seed]).standard_normal(out[name].shape)
        drawn = base * np.exp(spread * noise) if base else spread * noise
        out[name] = __import__('jax').numpy.asarray(drawn.astype(out[name].dtype))
    for name, factor in factors.items():
        out[name] = (out[name] * factor).astype(out[name].dtype)
    return out
```

```python
import math
from contextlib import ExitStack, contextmanager

import numpy as np

import concourse.bass as bass
from concourse import mybir

F32 = mybir.dt.float32
F32R = mybir.dt.float32r
ALU = mybir.AluOpType
ACT = mybir.ActivationFunctionType
AX = mybir.AxisListType

P = 128
D = 1024
KT = D // P
SEQ = 256
CTX = 256
DEPTH = 2
CONV_W = 512
CT = CONV_W // P
CONV_K = 31
TAPS_QK = 2
PAD = CONV_K // 2
ZW = SEQ + 2 * PAD
HEADS = 8
QK = 64
VD = 128
D_FF = 4 * D
GRID_W = 64
EPS = 1e-6
LN_EPS = 1e-5
ALPHA = (2 * DEPTH) ** 0.25

A_HEADS = 8
A_KV = 2
A_DH = 64
B_HEADS = 4
B_CONV = 4
B_CHUNK = 64
XT3 = 12
PAIRS = 2 * B_HEADS
LEVELS = 6
LRU_BLOCKS = 4
LRU_C = 8.0

CHUNK = 2048
CC = CHUNK // KT
RAW = 4
DB = 4
AB = 2
AHEAD = 2
FIRST_GEMM = KT + 1

ADA_CHUNKS = 6 * D // CC
ADA_FIRST = 2 * D // CC
FF_STEPS = D_FF // CC
HYB_TAIL = 2 * B_HEADS


def layout(sizes):
    at, out = 0, {}
    for name, n in sizes:
        out[name] = (at, n)
        at += n
    return out, at


COLS, COLS_N = layout([
    ("cond", 2 * KT), ("b_ada", DEPTH * 48), ("norm1_g", DEPTH * KT), ("norm2_g", DEPTH * KT),
    ("b_gate", DEPTH * 16), ("w_dw", DEPTH * CT * CONV_K), ("b_dw", DEPTH * CT), ("conv_ln_g", DEPTH * CT),
    ("conv_ln_b", DEPTH * CT), ("hyb_conv", XT3 * B_CONV), ("rec_conv", KT * B_CONV), ("rec_conv_b", KT),
    ("rec_b_a", KT), ("rec_b_x", KT), ("rec_lambda", KT), ("ln1_g", DEPTH * KT), ("ln1_b", DEPTH * KT),
    ("ln2_g", DEPTH * KT), ("ln2_b", DEPTH * KT)])
ROWS, ROWS_N = layout([
    ("q_norm_g", DEPTH * QK), ("k_norm_g", DEPTH * QK), ("attn_norm_g", DEPTH * VD), ("lam_q", DEPTH * 2 * QK),
    ("lam_k", DEPTH * 2 * QK), ("sinks", A_HEADS), ("a_log", B_HEADS), ("dt_bias", B_HEADS), ("hyb_norm_w", P)])
CONSTS, CONSTS_N = layout([
    ("ident", P), ("ones", P), ("eps", 2), ("sum4", 2), ("cos", 2 * QK), ("sin", 2 * QK),
    ("cos2", 2 * A_DH), ("sin2", 2 * A_DH)])
MASKS, MASKS_N = layout([
    ("before", P), ("own", P), ("tri", P), ("block", P), ("strict", P), ("strictT", P),
    ("level", LEVELS * P), ("levelT", LEVELS * P)])


def shape_constants():
    f = np.float32
    c = np.zeros((P, CONSTS_N), f)

    def put(to, table, name, value):
        at, n = table[name]
        to[:, at:at + n] = value

    put(c, CONSTS, "ident", np.eye(P))
    put(c, CONSTS, "ones", 1.0)
    put(c, CONSTS, "eps", np.array([EPS, LN_EPS]))
    put(c, CONSTS, "sum4", np.array([[float(i < 4 and i % 2 == v) for v in range(2)] for i in range(P)]))
    tok = np.arange(SEQ, dtype=f)
    nf = QK // 4
    inv = np.power(f(10000.0), -np.arange(nf, dtype=f) / f(nf)).astype(f)
    ang = np.concatenate([np.floor(tok / GRID_W)[:, None] * inv, (tok % GRID_W)[:, None] * inv], -1).astype(f)
    half = A_DH // 2
    inv2 = (f(10000.0) ** (-np.arange(half, dtype=f) / f(half))).astype(f)
    ang2 = (tok[:, None] * inv2[None, :]).astype(f)
    for a, cn, sn in ((ang, "cos", "sin"), (ang2, "cos2", "sin2")):
        cos, sin = np.cos(a), np.sin(a)
        two = lambda x: x.reshape(2, P, QK).transpose(1, 0, 2).reshape(P, 2 * QK)
        put(c, CONSTS, cn, two(np.concatenate([cos, cos], -1)))
        put(c, CONSTS, sn, two(np.concatenate([-sin, sin], -1)))
    m = np.zeros((P, MASKS_N), f)
    i, j = np.arange(P)[:, None], np.arange(P)[None, :]
    same = (i // B_CHUNK) == (j // B_CHUNK)
    put(m, MASKS, "own", np.where(j <= i, 0.0, -1e30))
    put(m, MASKS, "before", np.where(j > i, 0.0, -1e30))
    put(m, MASKS, "tri", same & (i <= j))
    put(m, MASKS, "block", same)
    put(m, MASKS, "strict", same & (i > j))
    put(m, MASKS, "strictT", same & (i < j))
    lv = [(i // (2 << l) == j // (2 << l)) & (i % (2 << l) >= (1 << l)) & (j % (2 << l) < (1 << l))
          for l in range(LEVELS)]
    put(m, MASKS, "level", np.concatenate(lv, 1))
    put(m, MASKS, "levelT", np.concatenate([x.T for x in lv], 1))
    return c, m


def chunk_plan():
    every = range(KT)
    plan = []

    def cols(name, l, c0, n, kts=every, width=CC):
        plan.extend((name, l, kts, range(c, c + width)) for c in range(c0, c0 + n * width, width))

    def mlp(w1, w2, l):
        up = [(w1, l, every, range(CC * s, CC * s + CC)) for s in range(FF_STEPS)]
        down = [(w2, l, range(2 * s, 2 * s + 2), range(D)) for s in range(FF_STEPS)]
        plan.append(up[0])
        for s in range(FF_STEPS):
            if s + 1 < FF_STEPS:
                plan.append(up[s + 1])
            plan.append(down[s])

    for l in range(DEPTH):
        if l == 0:
            cols("w_ada", l, 0, ADA_FIRST)
        for half in range(2):
            cols("w_in", l, half * CC, 1)
            cols("w_in", l, CONV_W + half * CC, 1)
        cols("w_in", l, D, 4)
        cols("w_in", l, 2 * D, 4)
        cols("w_in", l, 3 * D, 4)
        cols("w_ada", l, ADA_FIRST * CC, ADA_CHUNKS - ADA_FIRST)
        if l + 1 < DEPTH:
            cols("w_ada", l + 1, 0, ADA_FIRST)
        cols("w_conv_out", l, 0, 2, range(CT), 2 * CC)
        cols("w_in", l, 4 * D, 4)
        cols("w_attn_out", l, 0, 4)
        cols("w_in", l, 5 * D, 4)
        cols("w_out", l, 0, 4)
        mlp("w_mlp1", "w_mlp2", l)
    cols("hyb_w_in_2", 0, 0, 11)
    cols("hyb_w_out_2", 0, 0, 4)
    mlp("mlp_w1_2", "mlp_w2_2", 0)
    cols("rec_w_in_2", 0, 0, 4)
    plan.append(("rec_w_a_2", 0, None, None))
    plan.append(("rec_w_x_2", 0, None, None))
    cols("rec_w_in_2", 0, D, 4)
    cols("rec_w_out_2", 0, 0, 4)
    mlp("mlp_w1_2", "mlp_w2_2", 1)
    return plan


CHUNKS = len(chunk_plan())
CHUNK_OF_VALUES = [next(n for n, (name, at, _, c) in enumerate(chunk_plan())
                        if name == "w_in" and at == l and c.start == 3 * D) for l in range(DEPTH)]
CHUNK_OF_FILLS = [next(n for n, (name, at, _, c) in enumerate(chunk_plan())
                       if name == "w_ada" and at == l and c.start == ADA_FIRST * CC) for l in range(DEPTH)]


class Tally:

    def __init__(self, eng):
        self.eng, self.n, self.per, self.j = eng, {"g": FIRST_GEMM}, {}, None
        self.last = 0

    def at(self, key, ahead=0):
        v = self.n.get(key, 0) + ahead
        return v if self.j is None or not self.per.get(key) else self.j * self.per[key] + v

    def up(self, key, k=1):
        self.n[key] = self.n.get(key, 0) + k

    def one(self, key):
        self.up(key)
        return 1

    def next(self, key, k=1):
        self.up(key, k)
        return self.at(key)

    def slot(self, key, size, ahead=0):
        assert self.j is None or self.per.get(key, 0) % size == 0, key
        return (self.n.get(key, 0) + ahead) % size

    @contextmanager
    def loop(self, times, **per):
        start = dict(self.n)
        with self.eng.Fori(0, times) as j:
            self.j, self.per = j, per
            yield j
            for key in set(self.n) | set(per):
                assert self.n.get(key, 0) - start.get(key, 0) == per.get(key, 0), (key, per)
        self.j, self.per = None, {}
        for key, k in per.items():
            self.n[key] = start.get(key, 0) + k * times


def build_program(nc, a):
    with ExitStack() as ctx:
        def sb(name, shape, dt=F32):
            return ctx.enter_context(nc.sbuf_tensor(name, shape, dt))

        ring_at = -(-nc.sbuf_base // 64) * 64
        raw = sb("raw_weights", [P, RAW, CHUNK])
        w_lo = nc.alloc_sbuf_tensor_at("weights_lo", [P, RAW, CHUNK], F32R, offset=ring_at)
        w_hi = sb("weights_hi", [P, RAW, CHUNK], F32R)
        xT = sb("xT", [P, KT, SEQ + CTX])
        cols = sb("cols", [P, COLS_N])
        rows = sb("rows", [P, ROWS_N])
        consts = sb("consts", [P, CONSTS_N])
        cond_parts = sb("cond_parts", [P, KT, 4], F32R)
        cond = sb("cond", [P, KT, 2])
        mods = sb("mods", [P, DEPTH, 48, 2])
        gains = sb("gains", [P, 2, KT, 2])
        attn_gain = sb("attn_gain", [P, VD])
        lam = sb("lam", [P, 4])
        small = sb("small", [P, 64])
        ssq = sb("ssq", [P, 32])
        qprod = sb("qprod", [P, 2 * QK])
        osq_row = sb("osq_row", [P, VD])
        root = sb("root", [P, SEQ + CTX])

        ARENA = 112 * 1024
        arena_at = -(-nc.sbuf_base // 64) * 64

        def place(name, kib, shape, dt=F32):
            size = 4 * int(np.prod(shape[1:]))
            assert kib * 1024 + size <= ARENA, (name, kib, size)
            return nc.alloc_sbuf_tensor_at(name, shape, dt, offset=int(arena_at + kib * 1024))

        T2 = SEQ + CTX
        hH = place("h_hi", 0, [P, KT, T2], F32R)
        hL = place("h_lo", 16, [P, KT, T2], F32R)
        qT = place("qT", 32, [P, HEADS, T2])
        kT = place("kT", 48, [P, HEADS, T2])
        val = place("val", 64, [P, 4, D])
        mix = place("mix", 96, [P, KT, T2])
        staged_x = place("staged_x", 32, [P, 4, D])
        mod_rows = place("mod_rows", 32, [P, 2 * D])
        square = place("square", 48, [P, KT, T2])
        z = place("z", 80, [P, CT, 2, ZW])
        zc = place("zc", 89, [P, CT, T2])
        zsq = place("zsq", 97, [P, CT, T2])
        zH = place("z_hi", 80, [P, CT, T2], F32R)
        zL = place("z_lo", 88, [P, CT, T2], F32R)
        gate_z = place("gate_z", 104, [P, 2, T2])
        gate_c = place("gate_c", 64, [P, 2, T2])
        gate_a = place("gate_a", 32, [P, 2, T2])
        qs = place("qs", 97, [P, 2, 4, 256])
        qtmp = place("qtmp", 105, [P, 2, 256])
        qsq = place("qsq", 107, [P, 4, 256])
        ex = place("ex", 96, [P, 3, 2, T2])
        exT = place("exT", 108, [P, 2, T2])
        oH = place("o_hi", 48, [P, KT, T2], F32R)
        oL = place("o_lo", 64, [P, KT, T2], F32R)
        y = place("y", 80, [P, KT, T2])
        ff = place("ff", 32, [P, 2, T2])
        ffsq = place("ffsq", 36, [P, 2, 2, T2])
        ffH = place("ff_hi", 48, [P, 2, 2, T2], F32R)
        ffL = place("ff_lo", 56, [P, 2, 2, T2], F32R)
        gH = place("g_hi", 0, [P, KT, SEQ], F32R)
        gL = place("g_lo", 8, [P, KT, SEQ], F32R)
        masks = place("masks", 16, [P, MASKS_N])
        w8 = place("w8", 26, [P, KT, HYB_TAIL])
        qa = place("qa", 27, [P, 2, 768])
        qr = place("qr", 33, [P, 2, 640])
        qtmp2 = place("qtmp2", 38, [P, 2, 640])
        swS = place("sw_scores", 43, [P, A_HEADS, 256])
        swT = place("sw_scoresT", 51, [P, A_HEADS, 2, P])
        qaT = place("qaT", 59, [P, 4, SEQ])
        kaT = place("kaT", 63, [P, SEQ])
        oA = place("oA", 64, [P, 2, 512])
        cx = place("cx", 68, [P, XT3, SEQ + B_CONV - 1])
        cy = place("cy", 81, [P, XT3, SEQ])
        csq = place("csq", 93, [P, PAIRS, P])
        qtok = place("qtok", 68, [P, PAIRS, P])
        zt = place("zt", 101, [P, 2, 512])
        ut = place("ut", 105, [P, PAIRS, P])
        dsm = place("dsm", 109, [P, 256])
        ktok = place("ktok", 27, [P, PAIRS, P])
        vtok = place("vtok", 31, [P, PAIRS, P])
        kb = place("kb", 35, [P, PAIRS, P])
        expG = place("expG", 39, [P, PAIRS, P])
        eD = place("eD", 43, [P, PAIRS, P])
        eDT = place("eDT", 47, [P, PAIRS, P])
        bR = place("bR", 51, [P, PAIRS, P])
        am = place("am", 55, [P, PAIRS, P])
        amT = place("amT", 59, [P, PAIRS, P])
        tI = place("tI", 68, [P, PAIRS, P])
        tIT = place("tIT", 72, [P, PAIRS, P])
        mL = place("mL", 76, [P, PAIRS, P])
        qkT = place("qkT", 93, [P, PAIRS, P])
        ktail = place("ktail", 97, [P, PAIRS, P])
        uu = place("uu", 43, [P, PAIRS, P])
        wT = place("wT", 47, [P, PAIRS, P])
        vnew = place("vnew", 51, [P, 2, B_HEADS, P])
        state = place("state", 55, [P, B_HEADS, P])
        oB = place("oB", 59, [P, 2, 512])
        osq = place("osq", 76, [P, 2, 512])
        xr = place("xr", 16, [P, KT, SEQ + B_CONV - 1])
        xc = place("xc", 25, [P, KT, SEQ])
        xcH = place("xc_hi", 33, [P, KT, SEQ], F32R)
        xcL = place("xc_lo", 41, [P, KT, SEQ], F32R)
        ga = place("ga", 49, [P, KT, SEQ])
        gi = place("gi", 57, [P, KT, SEQ])
        gg = place("gg", 65, [P, KT, SEQ])
        gt = place("gt", 73, [P, KT, SEQ])
        g3 = place("g3", 81, [P, KT, SEQ])
        outrow = place("outrow", 64, [P, 2, D])

        def col(name, i=None):
            at, n = COLS[name]
            return cols[:, at:at + n] if i is None else cols[:, at + i:at + i + 1]

        def row(name, i0=0, n=None):
            at, m = ROWS[name]
            return rows[:, at + i0:at + i0 + (m if n is None else n)]

        def rows_of(name, l):
            n = ROWS[name][1] // DEPTH
            return row(name, l * n, n)

        def cols_of(name, i, n):
            at = COLS[name][0]
            return cols[:, at + i:at + i + n]

        def con(name):
            at, n = CONSTS[name]
            return consts[:, at:at + n]

        def msk(name):
            at, n = MASKS[name]
            return masks[:, at:at + n]

        ident, ones = con("ident"), con("ones")
        eps6, eps5 = con("eps")[:, 0:1], con("eps")[:, 1:2]

        psum = ctx.enter_context(nc.psum_tensor("psum", [P, 8, 512], F32))

        sem = {}

        def S(name):
            if name not in sem:
                sem[name] = ctx.enter_context(nc.semaphore(name))
            return sem[name]

        chunk_landed = [S(f"chunk_landed{i}") for i in range(RAW)]
        hi_done, lo_done = S("hi_done"), S("lo_done")
        chunk_used = S("chunk_used")
        gemm_done = S("gemm_done")
        d_free, a_free = S("d_free"), S("a_free")
        stage_pe, stage_act, stage_dve, stage_pool = (S(f"stage_{e}") for e in ("pe", "act", "dve", "pool"))
        loaded, x_loaded, masks_loaded, stored = S("loaded"), S("x_loaded"), S("masks_loaded"), S("stored")

        ada_saved = S("ada_saved")
        a_ready = S("a_ready")
        act_step = S("act_step")
        beta_ready = S("beta_ready")
        c8_ready = S("c8_ready")
        cond_ready = S("cond_ready")
        cond_silu = S("cond_silu")
        conv2 = S("conv2")
        conv_step = S("conv_step")
        cy_ready = S("cy_ready")
        decay_in = S("decay_in")
        decays = S("decays")
        dve_step = S("dve_step")
        exT_ready = S("exT_ready")
        ex_ready = S("ex_ready")
        ff_hi = S("ff_hi")
        ff_ready = S("ff_ready")
        ff_squared = S("ff_squared")
        gate_ready = S("gate_ready")
        gate_used = S("gate_used")
        gelu_ready = S("gelu_ready")
        gg_in = S("gg_in")
        grams = S("grams")
        growed = S("growed")
        gsum = S("gsum")
        h_hi = S("h_hi")
        h_ready = S("h_ready")
        hg_ready = S("hg_ready")
        inv = S("inv")
        inv_ready = S("inv_ready")
        lam_dots = S("lam_dots")
        lam_exps = S("lam_exps")
        level_ready = S("level_ready")
        logits = S("logits")
        logits_in = S("logits_in")
        masks_in = S("masks_in")
        mix_ready = S("mix_ready")
        mix_split = S("mix_split")
        mixed = S("mixed")
        mods_done = S("mods_done")
        nb_ready = S("nb_ready")
        o_root = S("o_root")
        o_saved = S("o_saved")
        o_scaled = S("o_scaled")
        o_split = S("o_split")
        ob_root = S("ob_root")
        ob_ssq = S("ob_ssq")
        out_ready = S("out_ready")
        outs = S("outs")
        pool_step = S("pool_step")
        pv = S("pv")
        qa_in = S("qa_in")
        qa_ready = S("qa_ready")
        qk_normed = S("qk_normed")
        qk_normed2 = S("qk_normed2")
        qk_ready = S("qk_ready")
        qk_root = S("qk_root")
        qk_ssq = S("qk_ssq")
        root_ready = S("root_ready")
        scores_done = S("scores_done")
        soft_exp = S("soft_exp")
        soft_in = S("soft_in")
        spread_done = S("spread_done")
        sqrt_ready = S("sqrt_ready")
        ssq_step = S("ssq_step")
        state_ready = S("state_ready")
        sums = S("sums")
        supd = S("supd")
        sw_max = S("sw_max")
        sw_ready = S("sw_ready")
        tanh_ready = S("tanh_ready")
        turned = S("turned")
        uw = S("uw")
        var_ready = S("var_ready")
        w_ready = S("w_ready")
        weightsT = S("weightsT")
        ws = S("ws")
        x_centered = S("x_centered")
        x_done = S("x_done")
        x_in = S("x_in")
        xc_split = S("xc_split")
        y_ready = S("y_ready")
        z_hi = S("z_hi")
        z_normed = S("z_normed")
        z_split = S("z_split")
        zc_centered = S("zc_centered")
        zc_ready = S("zc_ready")

        block = ctx.enter_context(nc.Block())
        LAYERS = [(0, 2), (1, 1)]

        def units_of(segs):
            return [(h, q) for h in range(HEADS) for q in range(2 * segs)]

        def fills_of(l):
            mt = CC // P
            here = [(l, mt * i) for i in range(ADA_FIRST, ADA_CHUNKS)]
            return here + ([(l + 1, mt * i) for i in range(ADA_FIRST)] if l + 1 < DEPTH else [])

        def fills_at(i, l, segs):
            n, f = len(units_of(segs)), len(fills_of(l))
            return (i + 1) * f // n - i * f // n if i < n else 0

        @block.sync
        def _(sp):
            sp.dma_start(cols[:, :], a["cols"]).then_inc(loaded, 16)
            sp.dma_start(consts[:, :], a["consts"]).then_inc(loaded, 16)
            sp.dma_start(staged_x[:, :, :], a["x_rows"]).then_inc(x_loaded, 16)
            for s in range(RAW):
                sp.dma_start(raw[:, s, :], a["weights"][s]).then_inc(chunk_landed[s], 16)
            sp.dma_start(rows[:, :], a["rows"]).then_inc(loaded, 16)
            with sp.Fori(1, CHUNKS // RAW) as j:
                for s in range(RAW):
                    sp.wait_ge(chunk_used, j * RAW + (s + 1 - RAW))
                    sp.dma_start(raw[:, s, :], a["weights"][j * RAW + s]).then_inc(chunk_landed[s], 16)
            for n in range(CHUNKS // RAW * RAW, CHUNKS):
                sp.wait_ge(chunk_used, n + 1 - RAW)
                sp.dma_start(raw[:, n % RAW, :], a["weights"][n]).then_inc(chunk_landed[n % RAW], 16)
            sp.wait_ge(out_ready, 4)
            sp.dma_start(a["out"], outrow[:, :, :]).then_inc(stored, 16)
            sp.wait_ge(stored, 16)

        @block.tensor
        def _(pe):
            t = Tally(pe)

            def end_stage():
                pe.drain().then_inc(stage_pe, t.one("stage"))
                pe.wait_ge(stage_act, t.at("stage"))
                pe.wait_ge(stage_dve, t.at("stage"))
                pe.wait_ge(stage_pool, t.at("stage"))

            mm = pe.matmul

            def open_chunk():
                pe.wait_ge(lo_done, t.at("chunk", 1))
                s = t.slot("chunk", RAW)
                t.up("chunk")
                return w_hi[:, s, :], w_lo[:, s, :]

            def d_bank():
                if not (t.j is None and t.n.get("d", 0) < DB):
                    pe.wait_ge(d_free, t.at("d", 1 - DB))
                b = t.slot("d", DB)
                t.up("d")
                return psum[:, b, :]

            def a_bank():
                if not (t.j is None and t.n.get("a", 0) < AB):
                    pe.wait_ge(a_free, t.at("a", 1 - AB))
                b = DB + t.slot("a", AB)
                t.up("a")
                return psum[:, b, :]

            def product(out, terms, chunk_ends):
                for i, (wh, wl, vh, vl, weights_stay) in enumerate(terms):
                    pair = (lambda w, v: (w, v)) if weights_stay else (lambda w, v: (v, w))
                    mm(out, *pair(wh, vh), start=i == 0, stop=False)
                    low = mm(out, *pair(wl, vh), start=False, stop=False)
                    last = mm(out, *pair(wh, vl), start=False, stop=i == len(terms) - 1)
                if chunk_ends:
                    low.then_inc(chunk_used, 1)
                last.then_inc(gemm_done, 1)
                t.up("g")

            def gemm_T(bank, H, L, T, kts=KT, mts=2, hk=0):
                wh, wl = (w.rearrange("p (k n) -> p k n", k=kts) for w in open_chunk())
                for m in range(mts):
                    out = bank()[:, 0:T]
                    c = slice(m * P, m * P + P)
                    product(out, [(wh[:, k, c], wl[:, k, c], H[:, hk + k, 0:T], L[:, hk + k, 0:T], True)
                                  for k in range(kts)], m == mts - 1)

            def gemm_M(bank, H, L, tts):
                wh, wl = (w.rearrange("p (k n) -> p k n", k=KT) for w in open_chunk())
                for tt in range(tts):
                    out = bank()[:, 0:CC]
                    c = slice(tt * P, tt * P + P)
                    product(out, [(wh[:, k, :], wl[:, k, :], H[:, k, c], L[:, k, c], False) for k in range(KT)],
                            tt == tts - 1)

            def column_sums(src, tiles, T, out, ready):
                for k in range(tiles):
                    if ready:
                        pe.wait_ge(S(ready), t.next(ready))
                    last = mm(out[:, 0:T], ones, src(k), start=k == 0, stop=k == tiles - 1)
                last.then_inc(sums, t.one("sums"))

            def moved_d():
                pe.wait_ge(d_free, t.at("d"))

            def moved_a():
                pe.wait_ge(a_free, t.at("a"))

            def mlp(T):
                def up():
                    gemm_T(a_bank, hH_, hL_, T)

                def down(par):
                    for i in range(2):
                        pe.wait_ge(ff_ready, t.next("ff_ready"))
                    wh, wl = (w.rearrange("p (k n) -> p k n", k=2) for w in open_chunk())
                    for m in range(KT):
                        out = d_bank()[:, 0:T]
                        c = slice(m * P, m * P + P)
                        product(out, [(wh[:, k, c], wl[:, k, c], ffH[:, par, k, 0:T], ffL[:, par, k, 0:T], True)
                                      for k in range(2)], m == KT - 1)

                up()
                with t.loop(FF_STEPS // 2 - 1, chunk=4, a=4, d=16, g=20, ff_ready=4):
                    up()
                    down(0)
                    up()
                    down(1)
                up()
                down(0)
                down(1)

            def modulation(out):
                wh, wl = (w.rearrange("p (k n) -> p k n", k=KT) for w in open_chunk())
                for k in range(KT):
                    low = mm(out, cond_parts[:, k, :], wl[:, k, :], start=k == 0, stop=False)
                    last = mm(out, cond_parts[:, k, :], wh[:, k, :], start=False, stop=k == KT - 1)
                low.then_inc(chunk_used, 1)
                last.then_inc(gemm_done, 1)
                t.up("g")

            pe.sem_inc(gemm_done, FIRST_GEMM)
            pe.wait_ge(x_in, t.next("x_in", 1))
            for k in range(KT):
                b = d_bank()
                for tt in range(4):
                    last = pe.transpose(b[:, tt * P:tt * P + P], staged_x[:, tt, k * P:k * P + P], ident)
                last.then_inc(turned, t.one("turned"))
            end_stage()

            for l, segs in LAYERS:
                TX, TA = segs * SEQ, SEQ + CTX
                hH_, hL_ = hH, hL
                if l == 0:
                    pe.wait_ge(cond_ready, t.next("cond_ready"))
                    with t.loop(ADA_FIRST // 4, chunk=4, d=4, g=4):
                        for _ in range(4):
                            modulation(d_bank()[0:4, 0:CC])
                    moved_d()
                    for n in range(2 * KT):
                        last = mm(psum[:, 6, 2 * n:2 * n + 2], mod_rows[0:4, n * P:n * P + P], con("sum4")[0:4, :],
                                  start=True, stop=True)
                    last.then_inc(mods_done, t.one("mods_done"))
                    end_stage()
                column_sums(lambda k: square[:, k, 0:TA], KT, TA, psum[:, 6, :], "square_ready")
                pe.wait_ge(h_ready, t.next("h_ready", KT))
                end_stage()
                for half in range(2):
                    gemm_T(d_bank, hH, hL, TX)
                    gemm_T(a_bank, hH, hL, TX)
                end_stage()
                def turn(c, tts):
                    pe.wait_ge(qk_ready, t.next("qk_ready"))
                    for h in range(2):
                        b = a_bank()
                        for tt in range(tts):
                            last = pe.transpose(b[:, tt * P:tt * P + P],
                                                qs[:, c % 2, tt, h * P:h * P + P], ident)
                        last.then_inc(turned, t.one("turned"))

                for c in range(8):
                    gemm_M(d_bank, hH, hL, 2 * segs if c < 4 else 4)
                    if c >= 1:
                        turn(c - 1, 2 * segs if c - 1 < 4 else 4)
                turn(7, 4)
                for c in range(4):
                    if c == 3:
                        column_sums(lambda k: zc[:, k, 0:TX], CT, TX, psum[:, 6, :], "zc_ready")
                    gemm_M(a_bank, hH, hL, 4)
                column_sums(lambda k: zsq[:, k, 0:TX], CT, TX, psum[:, 7, :], "zsq_ready")
                end_stage()
                units = units_of(segs)

                def keys(q):
                    return (0, 4) if q < 2 else (2, 4)

                def scores(u):
                    h, q = units[u]
                    k0, k1 = keys(q)
                    for c in range(2):
                        b = psum[:, 2 * (u % 2) + c, 0:(k1 - k0) * P]
                        if u >= 2 and c == 0:
                            pe.wait_ge(ex_ready, t.next("ex_ready"))
                        last = mm(b, qT[64 * c:64 * c + 64, h, q * P:q * P + P],
                                  kT[64 * c:64 * c + 64, h, k0 * P:k1 * P], start=True, stop=True)
                    last.then_inc(scores_done, t.one("scores_done"))

                def turn_weights(u):
                    h, q = units[u]
                    k0, k1 = keys(q)
                    pe.wait_ge(w_ready, t.next("w_ready"))
                    if u >= 1:
                        pe.wait_ge(exT_ready, t.at("exT_ready", 1))
                    b = psum[:, 4, :]
                    for i in range(k1 - k0):
                        last = pe.transpose(b[:, i * P:i * P + P], ex[:, u % 3, 0, i * P:i * P + P], ident)
                    last.then_inc(weightsT, t.one("weightsT"))

                def values(u):
                    h, q = units[u]
                    k0, k1 = keys(q)
                    pe.wait_ge(exT_ready, t.next("exT_ready"))
                    if u >= 2:
                        pe.wait_ge(o_saved, t.next("o_saved"))
                    for i in range(k1 - k0):
                        last = mm(psum[:, 6 + u % 2, 0:VD], exT[:, u % 2, i * P:i * P + P],
                                  val[:, k0 + i, h * VD:h * VD + VD], start=i == 0, stop=i == k1 - k0 - 1)
                    last.then_inc(pv, t.one("pv"))

                def spread_mods(f):
                    pe.wait_ge(ada_saved, t.next("ada_saved"))
                    for i in range(CC // P):
                        n = 256 + 2 * (f * (CC // P) + i)
                        last = mm(psum[:, 5, n:n + 2], root[0:4, i * P:i * P + P], con("sum4")[0:4, :],
                                  start=True, stop=True)
                    return last

                scores(0)
                scores(1)
                f = 0
                for i in range(len(units) + 2):
                    if i + 2 < len(units):
                        scores(i + 2)
                    if 1 <= i <= len(units):
                        turn_weights(i - 1)
                    if i >= 2:
                        values(i - 2)
                    if fills_at(i, l, segs):
                        if f >= 1:
                            spread_mods(f - 1)
                        modulation(psum[0:4, 5, 0:CC])
                        f += 1
                spread_mods(f - 1).then_inc(mods_done, t.one("mods_done"))
                t.up("ex_ready", 2)
                t.up("o_saved", 2)
                end_stage()
                for half in range(2):
                    gemm_T(d_bank, zH, zL, TX, kts=CT, mts=4)
                for c in range(4):
                    gemm_T(a_bank, hH, hL, TX)
                pe.wait_ge(o_scaled, t.next("o_scaled"))
                for h in range(HEADS):
                    b = d_bank()
                    for q in range(2 * segs):
                        last = pe.transpose(b[:, q * P:q * P + P], qT[:, h, q * P:q * P + P], ident)
                    last.then_inc(turned, t.one("turned"))
                moved_d()
                for c in range(4):
                    gemm_T(d_bank, oH, oL, TX)
                for c in range(4):
                    gemm_T(a_bank, hH, hL, TX)
                pe.wait_ge(mix_split, t.next("mix_split", KT))
                for c in range(4):
                    gemm_T(d_bank, oH, oL, TX)
                end_stage()
                column_sums(lambda k: square[:, k, 0:TX], KT, TX, psum[:, 6, :], "square_ready")
                pe.wait_ge(h_ready, t.next("h_ready", KT))
                mlp(TX)
                end_stage()

            def layer_norm():
                moved_d()
                column_sums(lambda k: xT[:, k, 0:SEQ], KT, SEQ, psum[:, 6, :], None)
                column_sums(lambda k: square[:, k, 0:SEQ], KT, SEQ, psum[:, 7, :], "square_ready")
                end_stage()

            def mlp2():
                pe.wait_ge(h_ready, t.next("h_ready", KT))
                mlp(SEQ)
                layer_norm()

            T = SEQ
            hH_, hL_ = gH, gL
            pe.wait_ge(h_ready, t.next("h_ready", KT))
            for c in range(3):
                gemm_M(d_bank, gH, gL, 2)
            for c in range(6):
                gemm_T(d_bank, gH, gL, T)
            for c in range(2):
                gemm_M(a_bank, gH, gL, 2)
            pe.wait_ge(masks_in, t.next("masks_in"))
            for tt in range(2):
                b = psum[:, 6, tt * HYB_TAIL:(tt + 1) * HYB_TAIL]
                for k in range(KT):
                    last = mm(b, xT[:, k, tt * P:tt * P + P], w8[:, k, :], start=k == 0, stop=k == KT - 1)
            last.then_inc(logits, t.one("logits"))
            pe.wait_ge(qa_ready, t.next("qa_ready"))
            for i in range(4):
                b = a_bank()
                for tt in range(2):
                    last = pe.transpose(b[:, tt * P:tt * P + P], qr[:, tt, i * P:i * P + P], ident)
                last.then_inc(turned, t.one("turned"))
            b = a_bank()
            for tt in range(2):
                last = pe.transpose(b[:, tt * P:tt * P + P], qr[:, tt, 512:640], ident)
            last.then_inc(turned, t.one("turned"))
            moved_a()
            for tt in range(2):
                nk = (tt + 1) * P
                for kv in range(A_KV):
                    for j in range(2):
                        b = d_bank()
                        r = slice(64 * kv, 64 * kv + 64)
                        for i in range(2):
                            last = mm(b[:, i * nk:i * nk + nk], qaT[r, 2 * j + i, tt * P:tt * P + P], kaT[r, 0:nk],
                                      start=True, stop=True)
                        last.then_inc(scores_done, t.one("scores_done"))
                pe.wait_ge(sw_ready, t.next("sw_ready"))
                for pair in range(4):
                    b = a_bank()
                    for kv in range(A_KV):
                        for i in range(tt + 1):
                            o = (kv * (tt + 1) + i) * P
                            last = pe.transpose(b[:, o:o + P], swS[:, 2 * pair + kv, i * P:i * P + P], ident)
                    last.then_inc(weightsT, t.one("weightsT"))
                moved_a()
                b = d_bank()
                for pair in range(4):
                    for kv in range(A_KV):
                        h = pair + 4 * kv
                        for i in range(tt + 1):
                            last = mm(b[:, h * 64:h * 64 + 64], swT[:, 2 * pair + kv, i, :],
                                      qa[:, i, 640 + 64 * kv:704 + 64 * kv], start=i == 0, stop=i == tt)
                last.then_inc(pv, t.one("pv"))
            end_stage()
            pe.wait_ge(cy_ready, t.next("cy_ready", XT3))
            for g in range(6):
                b = d_bank()
                for h in range(B_HEADS):
                    last = pe.transpose(b[:, h * P:h * P + P],
                                        cy[:, 4 * (g // 2) + h, (g % 2) * P:(g % 2) * P + P], ident)
                last.then_inc(turned, t.one("turned"))
            for g in range(4):
                if g % 2 == 0:
                    pe.wait_ge(qk_normed2, t.next("qk_normed2"))
                b = d_bank()
                for h in range(B_HEADS):
                    src = (qtok if g < 2 else ktok)[:, 4 * (g % 2) + h, :]
                    last = pe.transpose(b[:, h * P:h * P + P], src, ident)
                last.then_inc(turned, t.one("turned"))
            for tt in range(2):
                mm(psum[:, 6, tt * 4:tt * 4 + 4], msk("tri"), dsm[:, 8 + 4 * tt:12 + 4 * tt], start=True, stop=True)
                last = mm(psum[:, 6, 8 + tt * 4:12 + tt * 4], msk("block"), dsm[:, 8 + 4 * tt:12 + 4 * tt],
                          start=True, stop=True)
            last.then_inc(gsum, t.one("gsum"))
            pe.wait_ge(spread_done, t.next("spread_done"))
            for tt in range(2):
                b = d_bank()
                for h in range(4):
                    last = mm(b[:, h * P:h * P + P], eD[:, 4 * tt + h, :], msk("tri"), start=True, stop=True)
                last.then_inc(growed, t.one("growed"))
            for tt in range(2):
                b = d_bank()
                for h in range(4):
                    last = mm(b[:, h * P:h * P + P], eDT[:, 4 * tt + h, :], ident, start=True, stop=True)
                last.then_inc(growed, t.one("growed"))
            moved_d()
            for what in range(2):
                for tt in range(2):
                    b = d_bank()
                    r = slice(tt * P, tt * P + P)
                    for h in range(4):
                        last = mm(b[:, h * P:h * P + P], cy[:, 4 + h, r], cy[:, (4 if what == 0 else 0) + h, r],
                                  start=True, stop=True)
                    last.then_inc(grams, t.one("grams"))
            for l in range(1, LEVELS):
                pe.wait_ge(level_ready, t.next("level_ready"))
                for tt in range(2):
                    b = d_bank()
                    for h in range(4):
                        last = mm(b[:, h * P:h * P + P], mL[:, 4 * tt + h, :], tI[:, 4 * tt + h, :],
                                  start=True, stop=True)
                    last.then_inc(inv, t.one("inv"))
                moved_d()
                for tt in range(2):
                    b = d_bank()
                    for h in range(4):
                        last = mm(b[:, h * P:h * P + P], tIT[:, 4 * tt + h, :], ut[:, 4 * tt + h, :],
                                  start=True, stop=True)
                    last.then_inc(inv, t.one("inv"))
                for tt in range(2):
                    b = d_bank()
                    for h in range(4):
                        last = mm(b[:, h * P:h * P + P], ut[:, 4 * tt + h, :], tIT[:, 4 * tt + h, :],
                                  start=True, stop=True)
                    last.then_inc(inv, t.one("inv"))
            pe.wait_ge(inv_ready, t.next("inv_ready"))
            for what in range(2):
                for tt in range(2):
                    b = d_bank()
                    for h in range(4):
                        i = 4 * tt + h
                        if what == 0:
                            last = mm(b[:, h * P:h * P + P], tIT[:, i, :], vtok[:, i, :], start=True, stop=True)
                        else:
                            last = mm(b[:, h * P:h * P + P], kb[:, i, :], tIT[:, i, :], start=True, stop=True)
                    last.then_inc(uw, t.one("uw"))
            for c in range(SEQ // B_CHUNK):
                tt, half = c // 2, c % 2
                r = slice(64 * half, 64 * half + 64)
                if c == 0:
                    pe.wait_ge(state_ready, t.next("state_ready"))
                moved_d()
                b = d_bank()
                for h in range(4):
                    last = mm(b[:, h * P:h * P + P], wT[:, 4 * tt + h, :], state[:, h, :], start=True, stop=True)
                last.then_inc(ws, t.one("ws"))
                moved_d()
                b = d_bank()
                for h in range(4):
                    mm(b[:, h * P:h * P + P], cy[:, h, tt * P:tt * P + P], state[:, h, :], start=True, stop=False)
                    last = mm(b[:, h * P:h * P + P], qkT[:, 4 * tt + h, :], vnew[:, tt, h, :],
                              start=False, stop=True)
                last.then_inc(outs, t.one("outs"))
                if c + 1 < SEQ // B_CHUNK:
                    b = d_bank()
                    for h in range(4):
                        last = mm(b[:, h * P:h * P + P], ktail[r, 4 * tt + h, :], vnew[r, tt, h, :],
                                  start=True, stop=True)
                    last.then_inc(supd, t.one("supd"))
            pe.wait_ge(mixed, t.next("mixed"))
            for k in range(KT):
                b = d_bank()
                for tt in range(2):
                    src = (oA if k < 4 else oB)[:, tt, (k % 4) * P:(k % 4) * P + P]
                    last = pe.transpose(b[:, tt * P:tt * P + P], src, ident)
                last.then_inc(turned, t.one("turned"))
            moved_d()
            for c in range(4):
                gemm_T(d_bank, gH, gL, T)
            layer_norm()
            mlp2()
            pe.wait_ge(h_ready, t.next("h_ready", KT))
            for c in range(4):
                gemm_T(d_bank, gH, gL, T)
            pe.wait_ge(xc_split, t.next("xc_split", KT))
            for bank in (a_bank, a_bank):
                wh, wl = (w.rearrange("p (b n) -> p b n", b=KT) for w in open_chunk())
                for blk in range(LRU_BLOCKS):
                    for m in range(2):
                        c = slice(m * P, m * P + P)
                        product(bank()[:, 0:T], [(wh[:, 2 * blk + k, c], wl[:, 2 * blk + k, c],
                                                  xcH[:, 2 * blk + k, :], xcL[:, 2 * blk + k, :], True)
                                                 for k in range(2)], blk == LRU_BLOCKS - 1 and m == 1)
            for c in range(4):
                gemm_T(d_bank, gH, gL, T)
            pe.wait_ge(o_split, t.next("o_split", KT))
            for c in range(4):
                gemm_T(d_bank, xcH, xcL, T)
            layer_norm()
            mlp2()
            pe.wait_ge(x_done, t.next("x_done", 4))
            for g in range(4):
                b = d_bank()
                for k in range(4):
                    last = pe.transpose(b[:, k * P:k * P + P],
                                        xT[:, 4 * (g % 2) + k, (g // 2) * P:(g // 2) * P + P], ident)
                last.then_inc(turned, t.one("turned"))


        @block.scalar
        def _(act):
            t = Tally(act)

            def end_stage():
                act.drain().then_inc(stage_act, t.one("stage"))
                act.wait_ge(stage_pe, t.at("stage"))
                act.wait_ge(stage_dve, t.at("stage"))
                act.wait_ge(stage_pool, t.at("stage"))

            f = act.activation

            def next_hi():
                if t.n.get("chunk", 0) + AHEAD < CHUNKS:
                    s = t.slot("chunk", RAW, AHEAD)
                    n = t.n.get("chunk", 0) + AHEAD
                    v = 16 * (n // RAW + 1)
                    act.wait_ge(chunk_landed[s], v if t.j is None else t.j * (16 * t.per["chunk"] // RAW) + v)
                    act.wait_ge(gemm_done, t.at("g", -t.last))
                    f(w_hi[:, s, :], raw[:, s, :], ACT.Copy).then_inc(hi_done, 1)
                t.up("chunk")

            def chunk(tiles, evac=None):
                next_hi()
                t.last = tiles
                for i in range(tiles):
                    t.up("g")
                    if evac:
                        act.wait_ge(gemm_done, t.at("g"))
                        evac(i, a_result())

            def a_result():
                b = DB + t.slot("a", AB)
                t.up("a")
                return psum[:, b, :]

            def split_hi(dst, src, ready, done):
                act.wait_ge(S(ready), t.next(ready))
                f(dst, src, ACT.Copy).then_inc(S(done), t.one(done))

            def gate_tile(gate, b, bias, T):
                t.up("gate")
                if t.n["gate"] > 2:
                    act.wait_ge(gate_used, t.n["gate"] - 2)
                g = gate[:, (t.n["gate"] - 1) % 2, 0:T]
                f(g, b[:, 0:T], ACT.Sigmoid, **({"bias": bias} if bias is not None else {})).then_inc(gate_ready, t.one("gate_ready"))
                act.wait_ge(gate_ready, t.at("gate_ready"))
                act.sem_inc(a_free, 1)

            def squares(src, dst, tiles, ready, done):
                for k in range(tiles):
                    if ready:
                        act.wait_ge(S(ready), t.next(ready))
                    f(dst(k), src(k), ACT.Square).then_inc(S(done), t.one(done))

            def root_of(bank, T, n, eps):
                act.wait_ge(sums, t.next("sums"))
                f(root[:, 0:T], bank[:, 0:T], ACT.Sqrt, bias=eps, scale=1.0 / n).then_inc(root_ready, t.one("root_ready"))

            def mlp(T):
                def up(par):
                    next_hi()
                    t.last = 2
                    for m in range(2):
                        t.up("g")
                        act.wait_ge(gemm_done, t.at("g"))
                        b = a_result()
                        f(ff[:, m, 0:T], b[:, 0:T], ACT.Relu).then_inc(a_free, 1)
                    for m in range(2):
                        act.wait_ge(ff_squared, t.next("ff_squared"))
                        f(ffH[:, par, m, 0:T], ffsq[:, par, m, 0:T], ACT.Copy).then_inc(ff_hi, 1)

                up(0)
                t.last = KT
                with t.loop(FF_STEPS // 2 - 1, chunk=4, a=4, g=20, ff_squared=4):
                    up(1)
                    chunk(KT)
                    up(0)
                    chunk(KT)
                up(1)
                chunk(KT)
                chunk(KT)

            act.wait_ge(loaded, 16)
            act.wait_ge(loaded, 48)
            t.n["chunk"] = -AHEAD
            for _ in range(AHEAD):
                next_hi()
            f(cond[:, :, :].rearrange("p k v -> p (k v)"), col("cond"), ACT.Silu).then_inc(cond_silu, t.one("cond_silu"))
            end_stage()

            for l, segs in LAYERS:
                TX, TA = segs * SEQ, SEQ + CTX
                if l == 0:
                    t.last = 1
                    with t.loop(ADA_FIRST // 4, chunk=4, g=4):
                        for _ in range(4):
                            chunk(1)
                    end_stage()
                act.wait_ge(lam_dots, t.next("lam_dots"))
                f(lam[:, 2:4], lam[:, 0:2], ACT.Exp).then_inc(lam_exps, t.one("lam_exps"))
                squares(lambda k: xT[:, k, 0:TA], lambda k: square[:, k, 0:TA], KT, None, "square_ready")
                root_of(psum[:, 6, :], TA, D, eps6)
                for k in range(KT):
                    split_hi(hH[:, k, 0:TA], mix[:, k, 0:TA], "y_ready", "h_hi")
                end_stage()
                for half in range(2):
                    chunk(2)
                    chunk(2, lambda i, b: gate_tile(gate_z, b, None, TX))
                end_stage()
                def turned_qk(c):
                    to, T = (qT, TX) if c < 4 else (kT, TA)
                    for h in range(2):
                        act.wait_ge(turned, t.next("turned"))
                        f(to[:, 2 * (c % 4) + h, 0:T], a_result()[:, 0:T], ACT.Copy).then_inc(a_free, 1)

                t.n["turned"] = t.n.get("turned", 0) + (KT if l == 0 else HEADS)
                for c in range(8):
                    n = (2 * segs if c < 4 else 4)
                    chunk(n)
                    act.wait_ge(qk_ssq, t.next("qk_ssq"))
                    f(small[:, 16:16 + 4 * n], small[:, 0:4 * n], ACT.Sqrt, bias=eps6, scale=1.0 / QK).then_inc(qk_root, t.one("qk_root"))
                    if c >= 1:
                        turned_qk(c - 1)
                turned_qk(7)
                for c in range(4):
                    def keep(tt, b):
                        f(val[:, tt, c * CC:c * CC + CC], b[:, 0:CC], ACT.Copy).then_inc(a_free, 1)
                    if c == 3:
                        act.wait_ge(sums, t.next("sums"))
                        squares(lambda k: zc[:, k, 0:TX], lambda k: zsq[:, k, 0:TX], CT, "zc_centered", "zsq_ready")
                    chunk(4, keep)
                root_of(psum[:, 7, :], TX, CONV_W, eps6)
                for m in range(CT):
                    act.wait_ge(z_normed, t.next("z_normed"))
                    f(zsq[:, m, 0:TX], zc[:, m, 0:TX], ACT.Silu, bias=col("conv_ln_b", l * CT + m),
                      scale=col("conv_ln_g", l * CT + m)).then_inc(act_step, t.one("act_step"))
                    act.wait_ge(act_step, t.at("act_step"))
                    f(zH[:, m, 0:TX], zsq[:, m, 0:TX], ACT.Copy).then_inc(z_hi, t.one("z_hi"))
                end_stage()
                units = units_of(segs)

                def width(u):
                    return (4 if units[u][1] < 2 else 2) * P

                def exps(u):
                    act.wait_ge(nb_ready, t.next("nb_ready"))
                    for c in range(2):
                        last = f(ex[:, u % 3, c, 0:width(u)], psum[:, 2 * (u % 2) + c, 0:width(u)], ACT.Exp,
                                 bias=small[:, 36 + 2 * (u % 2) + c:37 + 2 * (u % 2) + c], scale=QK ** -0.5,
                                 accum_out=small[:, 40 + 2 * (u % 4) + c:41 + 2 * (u % 4) + c])
                    last.then_inc(ex_ready, t.one("ex_ready"))

                def keep_T(u):
                    act.wait_ge(weightsT, t.next("weightsT"))
                    if u >= 2:
                        act.wait_ge(pv, t.next("pv"))
                    f(exT[:, u % 2, 0:width(u)], psum[:, 4, 0:width(u)], ACT.Copy).then_inc(exT_ready, t.one("exT_ready"))

                def square_sum(u):
                    h, q = units[u]
                    act.wait_ge(o_saved, t.next("o_saved"))
                    if u >= 1:
                        act.wait_ge(ssq_step, t.at("ssq_step"))
                    f(osq_row[:, :], qT[:, h, q * P:q * P + P], ACT.Square, accum_out=ssq[:, u:u + 1])\
                        .then_inc(ssq_step, 1)
                    t.up("ssq_step")

                exps(0)
                for i in range(len(units) + 4):
                    if fills_at(i, l, segs):
                        chunk(1)
                    if i + 1 < len(units):
                        exps(i + 1)
                    if 1 <= i <= len(units):
                        keep_T(i - 1)
                    if i >= 4:
                        square_sum(i - 4)
                t.up("pv", 2)
                act.wait_ge(ssq_step, t.at("ssq_step"))
                f(ssq[:, 0:len(units)], ssq[:, 0:len(units)], ACT.Sqrt, bias=eps6, scale=1.0 / VD).then_inc(o_root, t.one("o_root"))
                end_stage()
                for half in range(2):
                    chunk(4)
                for c in range(4):
                    chunk(2, lambda i, b: gate_tile(gate_c, b, col("b_gate", l * 16 + 2 * c + i), TX))
                for c in range(4):
                    chunk(2)
                for c in range(4):
                    chunk(2, lambda i, b: gate_tile(gate_a, b, col("b_gate", l * 16 + 8 + 2 * c + i), TX))
                    for m in range(2 * c, 2 * c + 2):
                        split_hi(oH[:, m, 0:TX], mix[:, m, 0:TX], "mix_ready", "mix_hi")
                for c in range(4):
                    chunk(2)
                end_stage()
                squares(lambda k: xT[:, k, 0:TX], lambda k: square[:, k, 0:TX], KT, None, "square_ready")
                root_of(psum[:, 6, :], TX, D, eps6)
                for k in range(KT):
                    split_hi(hH[:, k, 0:TX], mix[:, k, 0:TX], "y_ready", "h_hi")
                mlp(TX)
                end_stage()

            def layer_norm():
                act.wait_ge(sums, t.next("sums"))
                squares(lambda k: xT[:, k, 0:SEQ], lambda k: square[:, k, 0:SEQ], KT, "x_centered", "square_ready")
                root_of(psum[:, 7, :], SEQ, D, eps5)
                end_stage()

            def split_x():
                for k in range(KT):
                    f(gH[:, k, :], xT[:, k, 0:SEQ], ACT.Copy).then_inc(h_hi, t.one("h_hi"))

            def mlp2():
                act.wait_ge(x_done, t.next("x_done"))
                split_x()
                mlp(SEQ)
                layer_norm()

            split_x()
            for c in range(3):
                chunk(2)
            for c in range(6):
                chunk(2)
            for c in range(2):
                def silu_z(tt, b):
                    f(zt[:, tt, c * CC:c * CC + CC], b[:, 0:CC], ACT.Silu).then_inc(a_free, 1)
                chunk(2, silu_z)
            t.n["turned"] = t.n["turned"] + HEADS
            for i in range(4):
                act.wait_ge(turned, t.next("turned"))
                f(qaT[:, i, :], a_result()[:, 0:SEQ], ACT.Copy).then_inc(a_free, 1)
            act.wait_ge(turned, t.next("turned"))
            f(kaT[:, :], a_result()[:, 0:SEQ], ACT.Copy).then_inc(a_free, 1)
            for tt in range(2):
                nk = (tt + 1) * P
                act.wait_ge(sw_max, t.next("sw_max"))
                for i in range(8):
                    f(swS[:, i, 0:nk], swS[:, i, 0:nk], ACT.Exp, bias=dsm[:, 72 + i:73 + i],
                      accum_out=dsm[:, 80 + i:81 + i])
                f(dsm[:, 96:104], dsm[:, 88:96], ACT.Exp).then_inc(sw_ready, t.one("sw_ready"))
                for pair in range(4):
                    act.wait_ge(weightsT, t.next("weightsT"))
                    n = 2 * (tt + 1)
                    f(swT[:, 2 * pair:2 * pair + 2, 0:tt + 1, :],
                      a_result()[:, 0:n * P].rearrange("p (v i q) -> p v i q", v=2, i=tt + 1),
                      ACT.Copy).then_inc(a_free, 1)
            act.wait_ge(logits_in, t.next("logits_in"))
            f(dsm[:, 0:8].rearrange("p (t h) -> p t h", t=2),
                     dsm[:, 32:48].rearrange("p (t h) -> p t h", t=2)[:, :, 0:4], ACT.Sigmoid).then_inc(beta_ready, t.one("beta_ready"))
            act.wait_ge(soft_in, t.next("soft_in"))
            f(dsm[:, 112:116], row("a_log"), ACT.Exp)
            f(dsm[:, 56:64], dsm[:, 48:56], ACT.Exp, scale=-1.0).then_inc(soft_exp, t.one("soft_exp"))
            end_stage()
            for i in range(XT3):
                act.wait_ge(conv2, t.next("conv2"))
                f(cy[:, i, :], cy[:, i, :], ACT.Silu).then_inc(cy_ready, t.one("cy_ready"))
            act.wait_ge(qk_ssq, t.next("qk_ssq"))
            f(dsm[:, 144:160], dsm[:, 128:144], ACT.Sqrt, bias=eps6).then_inc(qk_root, t.one("qk_root"))
            act.wait_ge(decay_in, t.next("decay_in"))
            flat = lambda x: x[:, :, :].rearrange("p i n -> p (i n)")
            f(flat(eD), flat(eD), ACT.Exp, scale=-1.0)
            f(flat(eDT), flat(eDT), ACT.Exp)
            f(dsm[:, 176:192], dsm[:, 160:176], ACT.Exp)
            f(flat(expG), flat(expG), ACT.Exp).then_inc(decays, t.one("decays"))
            act.wait_ge(ob_ssq, t.next("ob_ssq"))
            f(dsm[:, 200:208], dsm[:, 192:200], ACT.Sqrt, bias=eps6, scale=1.0 / P).then_inc(ob_root, t.one("ob_root"))
            for c in range(4):
                chunk(2)
            layer_norm()
            mlp2()
            act.wait_ge(x_done, t.next("x_done"))
            split_x()
            for c in range(4):
                chunk(2)
            act.wait_ge(soft_in, t.next("soft_in"))
            f(small[:, 56:64], small[:, 48:56], ACT.Exp, scale=-1.0).then_inc(soft_exp, t.one("soft_exp"))
            for k in range(KT):
                split_hi(xcH[:, k, :], xc[:, k, :], "xc_ready", "xc_hi")
            for g, bias in ((ga, "rec_b_a"), (gi, "rec_b_x")):
                def sig(i, b):
                    f(g[:, i, :], b[:, 0:SEQ], ACT.Sigmoid, bias=col(bias, i)).then_inc(a_free, 1)
                chunk(8, sig)
            for c in range(4):
                chunk(2)
            act.wait_ge(a_free, t.at("a"))
            act.wait_ge(c8_ready, t.next("c8_ready"))
            for k in range(KT):
                f(gt[:, k, :], ga[:, k, :], ACT.Tanh, scale=small[:, 40 + k:41 + k]).then_inc(tanh_ready, t.one("tanh_ready"))
            for k in range(KT):
                f(g3[:, k, :], ga[:, k, :], ACT.Exp, scale=small[:, 40 + k:41 + k]).then_inc(a_ready, t.one("a_ready"))
            for k in range(KT):
                act.wait_ge(var_ready, t.next("var_ready"))
                f(gt[:, k, :], gt[:, k, :], ACT.Sqrt, scale=-1.0).then_inc(sqrt_ready, t.one("sqrt_ready"))
            act.wait_ge(gg_in, t.next("gg_in"))
            for k in range(KT):
                f(gg[:, k, :], gg[:, k, :], ACT.Gelu_apprx_tanh).then_inc(gelu_ready, t.one("gelu_ready"))
            for k in range(KT):
                split_hi(xcH[:, k, :], xc[:, k, :], "hg_ready", "xc_hi")
            for c in range(4):
                chunk(2)
            layer_norm()
            mlp2()

        @block.vector
        def _(dve):
            t = Tally(dve)

            def end_stage():
                dve.drain().then_inc(stage_dve, t.one("stage"))
                dve.wait_ge(stage_pe, t.at("stage"))
                dve.wait_ge(stage_act, t.at("stage"))
                dve.wait_ge(stage_pool, t.at("stage"))

            tt_, ts, stt = dve.tensor_tensor, dve.tensor_scalar, dve.scalar_tensor_tensor

            def next_lo():
                if t.n.get("chunk", 0) + AHEAD < CHUNKS:
                    s = t.slot("chunk", RAW, AHEAD)
                    dve.wait_ge(hi_done, t.at("chunk", AHEAD + 1))
                    tt_(w_lo[:, s, :], raw[:, s, :], w_hi[:, s, :].bitcast(F32), ALU.subtract).then_inc(lo_done, 1)
                t.up("chunk")

            def d_result():
                b = t.slot("d", DB)
                t.up("d")
                return psum[:, b, :]

            def chunk(tiles, evac=None):
                next_lo()
                for i in range(tiles):
                    t.up("g")
                    if evac:
                        dve.wait_ge(gemm_done, t.at("g"))
                        evac(i, d_result()).then_inc(d_free, 1)

            def mine():
                dve.wait_ge(d_free, t.at("d"))

            def split_lo(dst, src, hi, ready, done):
                dve.wait_ge(S(ready), t.next(ready))
                tt_(dst, src, hi.bitcast(F32), ALU.subtract).then_inc(S(done), t.one(done))

            def recip(x):
                dve.reciprocal(x, x).then_inc(dve_step, t.one("dve_step"))
                dve.wait_ge(dve_step, t.at("dve_step"))

            def set_mods(l, n0, n, sums):
                tt_(mods[:, l, n0:n0 + n, :], sums.rearrange("p (n v) -> p n v", v=2),
                    cols_of("b_ada", l * 48 + n0, n).unsqueeze(2).to_broadcast([P, n, 2]),
                    ALU.add).then_inc(dve_step, t.one("dve_step"))
                dve.wait_ge(dve_step, t.at("dve_step"))

            def set_gain(l, which):
                name, at = (("norm1_g", KT), ("norm2_g", 4 * KT))[which]
                stt(gains[:, which, :, :], mods[:, l, at:at + KT, :], 1.0,
                    cols_of(name, l * KT, KT).unsqueeze(2).to_broadcast([P, KT, 2]),
                    ALU.add, ALU.mult).then_inc(dve_step, t.one("dve_step"))
                dve.wait_ge(dve_step, t.at("dve_step"))

            def modulated(T, l, which, shift):
                t.up("sums")
                dve.wait_ge(root_ready, t.next("root_ready"))
                recip(root[:, 0:T])
                for k in range(KT + 1):
                    if k < KT:
                        tt_(mix[:, k, 0:T], xT[:, k, 0:T], root[:, 0:T], ALU.mult).then_inc(dve_step, t.one("dve_step"))
                        dve.wait_ge(dve_step, t.at("dve_step"))
                        for v in range(T // SEQ):
                            c = slice(v * SEQ, v * SEQ + SEQ)
                            last = ts(mix[:, k, c], mix[:, k, c], gains[:, which, k, v:v + 1],
                                      mods[:, l, shift + k, v:v + 1], ALU.mult, ALU.add)
                        last.then_inc(y_ready, t.one("y_ready"))
                    if k >= 1:
                        split_lo(hL[:, k - 1, 0:T], mix[:, k - 1, 0:T], hH[:, k - 1, 0:T], "h_hi", "h_ready")
                dve.wait_ge(h_ready, t.at("h_ready"))

            def add_gated(m, b, T, l, which):
                for v in range(T // SEQ):
                    c = slice(v * SEQ, v * SEQ + SEQ)
                    last = stt(xT[:, m, c], b[:, c], mods[:, l, which + m, v:v + 1], xT[:, m, c], ALU.mult, ALU.add)
                return last

            def mlp(T, add):
                def sums():
                    for m in range(KT):
                        t.up("g")
                        dve.wait_ge(gemm_done, t.at("g"))
                        dve.wait_ge(d_free, t.at("d", 1 - KT))
                        add(m, d_result()).then_inc(d_free, 1)
                    next_lo()

                def down(par):
                    sums()
                    lows(par)

                def lows(par):
                    for m in range(2):
                        dve.wait_ge(ff_hi, t.next("ff_hi"))
                        tt_(ffL[:, par, m, 0:T], ffsq[:, par, m, 0:T], ffH[:, par, m, 0:T].bitcast(F32),
                                   ALU.subtract).then_inc(ff_ready, t.one("ff_ready"))

                chunk(2)
                lows(0)
                with t.loop(FF_STEPS // 2 - 1, chunk=4, d=16, g=20, ff_hi=4, ff_ready=4):
                    chunk(2)
                    down(1)
                    chunk(2)
                    down(0)
                chunk(2)
                down(1)
                sums()
                mine()

            def log1p_exp(e, s, s2, p, relu, out):
                ts(s, e, 2.0, None, ALU.add).then_inc(dve_step, t.one("dve_step"))
                dve.wait_ge(dve_step, t.at("dve_step"))
                recip(s)
                tt_(s, s, e, ALU.mult).then_inc(dve_step, t.one("dve_step"))
                dve.wait_ge(dve_step, t.at("dve_step"))
                tt_(s2, s, s, ALU.mult).then_inc(dve_step, t.one("dve_step"))
                dve.wait_ge(dve_step, t.at("dve_step"))
                ts(p, s2, 1.0 / 15, None, ALU.mult).then_inc(dve_step, t.one("dve_step"))
                dve.wait_ge(dve_step, t.at("dve_step"))
                for k in (13, 11, 9, 7, 5, 3):
                    stt(p, p, 1.0 / k, s2, ALU.add, ALU.mult).then_inc(dve_step, t.one("dve_step"))
                    dve.wait_ge(dve_step, t.at("dve_step"))
                stt(p, p, 1.0, s, ALU.add, ALU.mult).then_inc(dve_step, t.one("dve_step"))
                dve.wait_ge(dve_step, t.at("dve_step"))
                stt(out, p, 2.0, relu, ALU.mult, ALU.add).then_inc(dve_step, t.one("dve_step"))
                dve.wait_ge(dve_step, t.at("dve_step"))

            t.n["chunk"] = -AHEAD
            for _ in range(AHEAD):
                next_lo()
            dve.wait_ge(loaded, 48)
            dve.wait_ge(cond_silu, t.next("cond_silu"))
            dve.tensor_copy(cond_parts[:, :, 0:2], cond[:, :, :]).then_inc(dve_step, t.one("dve_step"))
            dve.wait_ge(dve_step, t.at("dve_step"))
            tt_(cond_parts[:, :, 2:4], cond[:, :, :], cond_parts[:, :, 0:2].bitcast(F32), ALU.subtract).then_inc(cond_ready, t.one("cond_ready"))
            for k in range(KT):
                dve.wait_ge(turned, t.next("turned"))
                b = d_result()
                dve.tensor_copy(xT[:, k, :], b).then_inc(d_free, 1)
            mine()
            end_stage()

            for l, segs in LAYERS:
                TX, TA = segs * SEQ, SEQ + CTX
                lam_init = 0.8 - 0.6 * math.exp(-0.3 * l)
                if l == 0:
                    with t.loop(ADA_FIRST // 4, chunk=4, d=4, g=4) as j:
                        for s in range(4):
                            chunk(1, lambda i, b: dve.tensor_copy(
                                mod_rows[0:4, bass.ds(j * (4 * CC) + s * CC, CC)], b[0:4, 0:CC]))
                    dve.wait_ge(mods_done, t.next("mods_done"))
                    set_mods(0, 0, 2 * KT, psum[:, 6, 0:4 * KT])
                    set_gain(0, 0)
                    end_stage()
                lq = rows_of("lam_q", l)
                tt_(qprod[:, :], lq, rows_of("lam_k", l), ALU.mult).then_inc(dve_step, t.one("dve_step"))
                dve.wait_ge(dve_step, t.at("dve_step"))
                dve.tensor_reduce(lam[:, 0:2], qprod[:, :].rearrange("p (a b) -> p a b", a=2), AX.X,
                                         ALU.add).then_inc(lam_dots, t.one("lam_dots"))
                dve.wait_ge(lam_exps, t.next("lam_exps"))
                tt_(lam[:, 0:1], lam[:, 3:4], lam[:, 2:3], ALU.subtract).then_inc(dve_step, t.one("dve_step"))
                dve.wait_ge(dve_step, t.at("dve_step"))
                ts(lam[:, 0:1], lam[:, 0:1], -lam_init, None, ALU.add).then_inc(dve_step, t.one("dve_step"))
                dve.wait_ge(dve_step, t.at("dve_step"))
                ts(attn_gain[:, :], row("attn_norm_g", l * VD, VD), 1.0 - lam_init, None, ALU.mult).then_inc(dve_step, t.one("dve_step"))
                dve.wait_ge(dve_step, t.at("dve_step"))
                modulated(TA, l, 0, 0)
                end_stage()
                dve.memset(z[:, :, :, 0:PAD], 0.0).then_inc(dve_step, t.one("dve_step"))
                dve.wait_ge(dve_step, t.at("dve_step"))
                dve.memset(z[:, :, :, PAD + SEQ:ZW], 0.0).then_inc(dve_step, t.one("dve_step"))
                dve.wait_ge(dve_step, t.at("dve_step"))
                two = lambda x: x.rearrange("p (s n) -> p s n", n=SEQ)
                for half in range(2):
                    chunk(2, lambda m, b: dve.tensor_copy(z[:, 2 * half + m, 0:segs, PAD:PAD + SEQ],
                                                          two(b[:, 0:TX])))
                    mine()
                    chunk(2)
                    for m in range(2):
                        zz = z[:, 2 * half + m, 0:segs, PAD:PAD + SEQ]
                        dve.wait_ge(gate_ready, t.next("gate_ready"))
                        tt_(zz, zz, two(gate_z[:, t.n.get("gate", 0) % 2, 0:TX]), ALU.mult).then_inc(gate_used, t.one("gate_used"))
                        t.up("gate")
                end_stage()

                def conv_taps(first, end):
                    for tap in range(first, end):
                        final = tap == CONV_K - 1
                        for m in range(CT):
                            o, i = two(zc[:, m, 0:TX]), z[:, m, 0:segs, tap:tap + SEQ]
                            wc = col("w_dw", (l * CT + m) * CONV_K + tap)
                            if tap == 0:
                                ins = ts(o, i, wc, col("b_dw", l * CT + m), ALU.mult, ALU.add)
                            else:
                                dve.wait_ge(conv_step, t.at("conv_step", -(CT - 1 - (m if final else 0))))
                                ins = stt(o, i, wc, o, ALU.mult, ALU.add)
                            if final:
                                ins.then_inc(zc_ready, t.one("zc_ready"))
                            else:
                                ins.then_inc(conv_step, t.one("conv_step"))

                t.n["turned"] = KT + l * (16 + HEADS) if l == 0 else t.n["turned"]
                for c in range(8):
                    n = (2 * segs if c < 4 else 4)
                    if c >= 2:
                        dve.wait_ge(turned, t.next("turned", 2))
                    q = qs[:, c % 2, 0:n, :]
                    chunk(n, lambda tt, b: dve.tensor_copy(qs[:, c % 2, tt, :], b[:, 0:CC]))
                    mine()
                    tt_(qsq[:, 0:n, :], q, q, ALU.mult).then_inc(dve_step, t.one("dve_step"))
                    dve.wait_ge(dve_step, t.at("dve_step"))
                    dve.tensor_reduce(small[:, 0:4 * n], qsq[:, 0:n, :].rearrange("p t (g d) -> p (t g) d", d=QK),
                                             AX.X, ALU.add).then_inc(qk_ssq, t.one("qk_ssq"))
                    dve.wait_ge(qk_root, t.next("qk_root"))
                    recip(small[:, 16:16 + 4 * n])
                    g = q.rearrange("p t (g d) -> p (t g) d", d=QK)
                    tt_(g, g, small[:, 16:16 + 4 * n].unsqueeze(2).to_broadcast([P, 4 * n, QK]), ALU.mult).then_inc(qk_normed, t.one("qk_normed"))
                    conv_taps(TAPS_QK * c, TAPS_QK * (c + 1))
                t.up("turned", 4)
                t.up("chunk", 4)
                t.up("g", 16)
                conv_taps(8 * TAPS_QK, CONV_K)
                dve.wait_ge(sums, t.next("sums"))
                for m in range(CT):
                    stt(zc[:, m, 0:TX], psum[:, 6, 0:TX], -1.0 / CONV_W, zc[:, m, 0:TX], ALU.mult, ALU.add).then_inc(zc_centered, t.one("zc_centered"))
                dve.wait_ge(root_ready, t.next("root_ready"))
                t.up("sums")
                recip(root[:, 0:TX])
                for m in range(CT):
                    tt_(zc[:, m, 0:TX], zc[:, m, 0:TX], root[:, 0:TX], ALU.mult).then_inc(z_normed, t.one("z_normed"))
                for m in range(CT):
                    split_lo(zL[:, m, 0:TX], zsq[:, m, 0:TX], zH[:, m, 0:TX], "z_hi", "z_split")
                end_stage()
                units = units_of(segs)

                def width(u):
                    return (4 if units[u][1] < 2 else 2) * P

                def maxima(u):
                    dve.wait_ge(scores_done, t.next("scores_done"))
                    m, nb = small[:, 32 + 2 * (u % 2):34 + 2 * (u % 2)], small[:, 36 + 2 * (u % 2):38 + 2 * (u % 2)]
                    dve.tensor_reduce(m, psum[:, 2 * (u % 2):2 * (u % 2) + 2, 0:width(u)], AX.X, ALU.max).then_inc(dve_step, t.one("dve_step"))
                    dve.wait_ge(dve_step, t.at("dve_step"))
                    ts(nb, m, -(QK ** -0.5), None, ALU.mult).then_inc(nb_ready, t.one("nb_ready"))

                def weights(u):
                    dve.wait_ge(ex_ready, t.next("ex_ready"))
                    b = 40 + 2 * (u % 4)
                    w0, w1 = ex[:, u % 3, 0, 0:width(u)], ex[:, u % 3, 1, 0:width(u)]
                    recip(small[:, b:b + 2])
                    tt_(small[:, b + 1:b + 2], small[:, b + 1:b + 2], lam[:, 0:1], ALU.mult).then_inc(dve_step, t.one("dve_step"))
                    dve.wait_ge(dve_step, t.at("dve_step"))
                    ts(w0, w0, small[:, b:b + 1], None, ALU.mult).then_inc(dve_step, t.one("dve_step"))
                    dve.wait_ge(dve_step, t.at("dve_step"))
                    stt(w0, w1, small[:, b + 1:b + 2], w0, ALU.mult, ALU.add).then_inc(w_ready, t.one("w_ready"))

                def save(u):
                    h, q = units[u]
                    dve.wait_ge(pv, t.next("pv"))
                    dve.tensor_copy(qT[:, h, q * P:q * P + P], psum[:, 6 + u % 2, 0:VD]).then_inc(o_saved, t.one("o_saved"))

                maxima(0)
                for i in range(len(units) + 3):
                    if i + 1 < len(units):
                        maxima(i + 1)
                    if i < len(units):
                        weights(i)
                    if i >= 3:
                        save(i - 3)
                    if i >= 1 and fills_at(i - 1, l, segs):
                        dve.wait_ge(gemm_done, t.at("g"))
                        dve.tensor_copy(root[0:4, 0:CC], psum[0:4, 5, 0:CC]).then_inc(ada_saved, 1)
                    if fills_at(i, l, segs):
                        t.up("g")
                        t.up("chunk")
                dve.wait_ge(mods_done, t.next("mods_done"))
                here = 2 * (6 * KT - 2 * KT)
                set_mods(l, 2 * KT, 4 * KT, psum[:, 5, 256:256 + here])
                set_gain(l, 1)
                if l + 1 < DEPTH:
                    set_mods(l + 1, 0, 2 * KT, psum[:, 5, 256 + here:256 + here + 4 * KT])
                    set_gain(l + 1, 0)
                end_stage()
                dve.wait_ge(o_root, t.next("o_root"))
                recip(ssq[:, 0:len(units)])
                dve.wait_ge(dve_step, t.at("dve_step"))

                def conv_out(n, b):
                    for u in range(2 * segs * n, 2 * segs * (n + 1)):
                        h, q = units[u]
                        o = qT[:, h, q * P:q * P + P]
                        ins = stt(o, o, ssq[:, u:u + 1], attn_gain[:, :], ALU.mult, ALU.mult)
                    if u == len(units) - 1:
                        ins.then_inc(o_scaled, t.one("o_scaled"))
                    return dve.tensor_copy(mix[:, n, 0:TX], b[:, 0:TX])

                for half in range(2):
                    chunk(4, lambda m, b: conv_out(4 * half + m, b))
                mine()
                for c in range(4):
                    chunk(2)
                    for m in range(2 * c, 2 * c + 2):
                        dve.wait_ge(gate_ready, t.next("gate_ready"))
                        tt_(mix[:, m, 0:TX], mix[:, m, 0:TX], gate_c[:, t.n["gate"] % 2, 0:TX], ALU.mult).then_inc(gate_used, t.one("gate_used"))
                        t.up("gate")
                dve.wait_ge(gate_used, t.at("gate_used"))
                for h in range(HEADS):
                    dve.wait_ge(turned, t.next("turned"))
                    b = d_result()
                    dve.tensor_copy(oH[:, h, 0:TX], b[:, 0:TX]).then_inc(dve_step, t.one("dve_step"))
                    dve.wait_ge(dve_step, t.at("dve_step"))
                    tt_(oL[:, h, 0:TX], b[:, 0:TX], oH[:, h, 0:TX].bitcast(F32), ALU.subtract).then_inc(d_free, 1)
                for c in range(4):
                    chunk(2, lambda m, b: dve.tensor_copy(y[:, 2 * c + m, 0:TX], b[:, 0:TX]))
                mine()
                for c in range(4):
                    chunk(2)
                    for m in range(2 * c, 2 * c + 2):
                        dve.wait_ge(gate_ready, t.next("gate_ready"))
                        tt_(y[:, m, 0:TX], y[:, m, 0:TX], gate_a[:, t.n["gate"] % 2, 0:TX], ALU.mult).then_inc(gate_used, t.one("gate_used"))
                        dve.wait_ge(gate_used, t.at("gate_used"))
                        t.up("gate")
                        tt_(mix[:, m, 0:TX], mix[:, m, 0:TX], y[:, m, 0:TX], ALU.add).then_inc(mix_ready, t.one("mix_ready"))
                    for m in range(2 * c, 2 * c + 2):
                        split_lo(oL[:, m, 0:TX], mix[:, m, 0:TX], oH[:, m, 0:TX], "mix_hi", "mix_split")
                for c in range(4):
                    chunk(2, lambda m, b: add_gated(2 * c + m, b, TX, l, 2 * KT))
                mine()
                end_stage()
                modulated(TX, l, 1, 3 * KT)
                mlp(TX, lambda m, b: add_gated(m, b, TX, l, 5 * KT))
                end_stage()

            def layer_norm(i, g, b):
                mine()
                dve.wait_ge(sums, t.next("sums"))
                for k in range(KT):
                    stt(xT[:, k, 0:SEQ], psum[:, 6, 0:SEQ], -1.0 / D, xT[:, k, 0:SEQ], ALU.mult, ALU.add).then_inc(x_centered, t.one("x_centered"))
                dve.wait_ge(root_ready, t.next("root_ready"))
                recip(root[:, 0:SEQ])
                t.up("sums")
                end_stage()
                for k in range(KT):
                    tt_(xT[:, k, 0:SEQ], xT[:, k, 0:SEQ], root[:, 0:SEQ], ALU.mult).then_inc(dve_step, t.one("dve_step"))
                    dve.wait_ge(dve_step, t.at("dve_step"))
                    last = ts(xT[:, k, 0:SEQ], xT[:, k, 0:SEQ], col(g, i * KT + k), col(b, i * KT + k),
                              ALU.mult, ALU.add)
                last.then_inc(x_done, t.one("x_done"))
                dve.wait_ge(x_done, t.at("x_done"))

            def split_x():
                for k in range(KT):
                    split_lo(gL[:, k, :], xT[:, k, 0:SEQ], gH[:, k, :], "h_hi", "h_ready")

            def mlp2(i):
                split_x()
                dve.wait_ge(h_ready, t.at("h_ready"))
                ts(xT[:, :, 0:SEQ], xT[:, :, 0:SEQ], ALPHA, None, ALU.mult).then_inc(dve_step, t.one("dve_step"))
                dve.wait_ge(dve_step, t.at("dve_step"))
                mlp(SEQ, lambda m, b: tt_(xT[:, m, 0:SEQ], b[:, 0:SEQ], xT[:, m, 0:SEQ], ALU.add))
                layer_norm(i, "ln2_g", "ln2_b")

            def add_scaled(m, b):
                return stt(xT[:, m, 0:SEQ], xT[:, m, 0:SEQ], ALPHA, b[:, 0:SEQ], ALU.mult, ALU.add)

            def causal(src, dst, tiles, w, bias, done):
                for tap in range(B_CONV):
                    for i in range(tiles):
                        wc = col(w, i * B_CONV + tap)
                        x = src[:, i, tap:tap + SEQ]
                        if tap == 0:
                            if bias:
                                ins = ts(dst[:, i, :], x, wc, col(bias, i), ALU.mult, ALU.add)
                            else:
                                ins = ts(dst[:, i, :], x, wc, None, ALU.mult)
                        else:
                            dve.wait_ge(dve_step, base + (tap - 1) * tiles + i + 1)
                            ins = stt(dst[:, i, :], x, wc, dst[:, i, :], ALU.mult, ALU.add)
                        if tap == 0 and i == 0:
                            base = t.n["dve_step"]
                        ins.then_inc(S(done if tap == B_CONV - 1 else "dve_step"), t.one(done if tap == B_CONV - 1 else "dve_step"))

            split_x()
            for c in range(3):
                chunk(2, lambda tt, b: dve.tensor_copy(qa[:, tt, c * CC:c * CC + CC], b[:, 0:CC]))
            mine()
            dve.memset(cx[:, :, 0:B_CONV - 1], 0.0).then_inc(qa_in, t.one("qa_in"))
            for c in range(6):
                chunk(2, lambda m, b: dve.tensor_copy(cx[:, 2 * c + m, B_CONV - 1:], b[:, 0:SEQ]))
            for c in range(2):
                chunk(2)
            dve.wait_ge(logits, t.next("logits"))
            dve.tensor_copy(dsm[:, 32:48], psum[:, 6, 0:16]).then_inc(logits_in, t.one("logits_in"))
            dve.wait_ge(logits_in, t.at("logits_in"))
            v24 = lambda x: x.rearrange("p (t h) -> p t h", t=2)
            dt = row("dt_bias").unsqueeze(1).to_broadcast([P, 2, 4])
            tt_(v24(dsm[:, 48:56]), v24(dsm[:, 32:48])[:, :, 4:8], dt, ALU.add).then_inc(dve_step, t.one("dve_step"))
            dve.wait_ge(dve_step, t.at("dve_step"))
            ts(dsm[:, 120:128], dsm[:, 48:56], 0.0, None, ALU.max).then_inc(dve_step, t.one("dve_step"))
            dve.wait_ge(dve_step, t.at("dve_step"))
            ts(dsm[:, 56:64], dsm[:, 48:56], -1.0, None, ALU.mult).then_inc(dve_step, t.one("dve_step"))
            dve.wait_ge(dve_step, t.at("dve_step"))
            tt_(dsm[:, 48:56], dsm[:, 48:56], dsm[:, 56:64], ALU.max).then_inc(soft_in, t.one("soft_in"))
            wrow = masks[:, MASKS["before"][0]:MASKS["before"][0] + 2 * P]
            for tt in range(2):
                nk = (tt + 1) * P
                mrow = wrow[:, 2 * P - nk:].unsqueeze(1).to_broadcast([P, 2, nk])
                if tt == 0:
                    dve.wait_ge(masks_loaded, 32)
                sw = swS[:, :, :].rearrange("p (a v) n -> p a v n", v=2)
                for kv in range(A_KV):
                    for j in range(2):
                        dve.wait_ge(scores_done, t.next("scores_done"))
                        b = d_result()
                        stt(
                            sw[:, 2 * j:2 * j + 2, kv, 0:nk], b[:, 0:2 * nk].rearrange("p (i n) -> p i n", i=2),
                            A_DH ** -0.5, mrow, ALU.mult, ALU.add).then_inc(d_free, 1)
                mine()
                dve.tensor_reduce(dsm[:, 64:72], swS[:, :, 0:nk], AX.X, ALU.max).then_inc(dve_step, t.one("dve_step"))
                dve.wait_ge(dve_step, t.at("dve_step"))
                tt_(dsm[:, 64:72], dsm[:, 64:72], row("sinks"), ALU.max).then_inc(dve_step, t.one("dve_step"))
                dve.wait_ge(dve_step, t.at("dve_step"))
                ts(dsm[:, 72:80], dsm[:, 64:72], -1.0, None, ALU.mult).then_inc(dve_step, t.one("dve_step"))
                dve.wait_ge(dve_step, t.at("dve_step"))
                tt_(dsm[:, 88:96], row("sinks"), dsm[:, 72:80], ALU.add).then_inc(sw_max, t.one("sw_max"))
                dve.wait_ge(sw_ready, t.next("sw_ready"))
                tt_(dsm[:, 104:112], dsm[:, 80:88], dsm[:, 96:104], ALU.add).then_inc(dve_step, t.one("dve_step"))
                dve.wait_ge(dve_step, t.at("dve_step"))
                recip(dsm[:, 104:112])
                r = dsm[:, 104:112].rearrange("p (a v) -> p v a", v=2).unsqueeze(3).to_broadcast([P, 2, 4, 64])
                dve.wait_ge(pv, t.next("pv"))
                b = d_result()
                tt_(oA[:, tt, :].rearrange("p (v a d) -> p v a d", v=2, a=4),
                                              b.rearrange("p (v a d) -> p v a d", v=2, a=4), r, ALU.mult).then_inc(d_free, 1)
            dve.wait_ge(beta_ready, t.next("beta_ready"))
            dve.wait_ge(soft_exp, t.next("soft_exp"))
            log1p_exp(dsm[:, 56:64], dsm[:, 210:218], dsm[:, 218:226], dsm[:, 226:234], dsm[:, 120:128],
                      dsm[:, 234:242])
            stt(v24(dsm[:, 8:16]), v24(dsm[:, 234:242]), -1.0,
                     dsm[:, 112:116].unsqueeze(1).to_broadcast([P, 2, 4]), ALU.mult, ALU.mult).then_inc(dve_step, t.one("dve_step"))
            dve.wait_ge(dve_step, t.at("dve_step"))
            end_stage()
            causal(cx, cy, XT3, "hyb_conv", None, "conv2")
            t.n["turned"] = t.n["turned"] + 5
            pairs = lambda x: x.rearrange("p (i n) -> p i n", n=P)
            spread = lambda c: c.unsqueeze(2).to_broadcast([P, PAIRS, P])
            every = lambda m: m.unsqueeze(1).to_broadcast([P, PAIRS, P])
            quad = lambda b: b.rearrange("p (h n) -> p h n", n=P)
            for to in (qtok, ktok, vtok):
                for tt in range(2):
                    dve.wait_ge(turned, t.next("turned"))
                    b = d_result()
                    dve.tensor_copy(to[:, 4 * tt:4 * tt + 4, :], quad(b)).then_inc(d_free, 1)
            mine()
            tt_(csq[:, :, :], qtok[:, :, :], qtok[:, :, :], ALU.mult).then_inc(dve_step, t.one("dve_step"))
            dve.wait_ge(dve_step, t.at("dve_step"))
            dve.tensor_reduce(dsm[:, 128:136], csq[:, :, :], AX.X, ALU.add).then_inc(dve_step, t.one("dve_step"))
            dve.wait_ge(dve_step, t.at("dve_step"))
            tt_(csq[:, :, :], ktok[:, :, :], ktok[:, :, :], ALU.mult).then_inc(dve_step, t.one("dve_step"))
            dve.wait_ge(dve_step, t.at("dve_step"))
            dve.tensor_reduce(dsm[:, 136:144], csq[:, :, :], AX.X, ALU.add).then_inc(qk_ssq, t.one("qk_ssq"))
            dve.wait_ge(qk_root, t.next("qk_root"))
            recip(dsm[:, 144:160])
            tt_(qtok[:, :, :], qtok[:, :, :], spread(dsm[:, 144:152]), ALU.mult).then_inc(qk_normed2, t.one("qk_normed2"))
            tt_(ktok[:, :, :], ktok[:, :, :], spread(dsm[:, 152:160]), ALU.mult).then_inc(qk_normed2, t.one("qk_normed2"))
            tt_(vtok[:, :, :], vtok[:, :, :], spread(dsm[:, 0:8]), ALU.mult).then_inc(dve_step, t.one("dve_step"))
            dve.wait_ge(dve_step, t.at("dve_step"))
            tt_(eD[:, :, :], every(ones), spread(dsm[:, 8:16]), ALU.mult).then_inc(dve_step, t.one("dve_step"))
            dve.wait_ge(dve_step, t.at("dve_step"))
            tt_(eDT[:, :, :], every(ones), spread(dsm[:, 0:8]), ALU.mult).then_inc(spread_done, t.one("spread_done"))
            for g in range(4):
                dve.wait_ge(turned, t.next("turned"))
                b = d_result()
                dve.tensor_copy(
                    cy[:, 4 * (g // 2):4 * (g // 2) + 4, (g % 2) * P:(g % 2) * P + P], quad(b)).then_inc(d_free, 1)
            dve.wait_ge(gsum, t.next("gsum"))
            dve.tensor_copy(dsm[:, 16:32], psum[:, 6, 0:16]).then_inc(dve_step, t.one("dve_step"))
            dve.wait_ge(dve_step, t.at("dve_step"))
            for tt in range(2):
                dve.wait_ge(growed, t.next("growed"))
                b = d_result()
                dve.tensor_copy(expG[:, 4 * tt:4 * tt + 4, :], quad(b)).then_inc(d_free, 1)
            for tt in range(2):
                dve.wait_ge(growed, t.next("growed"))
                b = d_result()
                dve.tensor_copy(bR[:, 4 * tt:4 * tt + 4, :], quad(b)).then_inc(d_free, 1)
            mine()
            tt_(eDT[:, :, :], expG[:, :, :], spread(dsm[:, 16:24]), ALU.subtract).then_inc(dve_step, t.one("dve_step"))
            dve.wait_ge(dve_step, t.at("dve_step"))
            ts(eD[:, :, :], eDT[:, :, :], 0.0, None, ALU.max).then_inc(dve_step, t.one("dve_step"))
            dve.wait_ge(dve_step, t.at("dve_step"))
            ts(eDT[:, :, :], eDT[:, :, :], 0.0, None, ALU.min).then_inc(dve_step, t.one("dve_step"))
            dve.wait_ge(dve_step, t.at("dve_step"))
            dve.tensor_copy(dsm[:, 160:168], dsm[:, 16:24]).then_inc(dve_step, t.one("dve_step"))
            dve.wait_ge(dve_step, t.at("dve_step"))
            tt_(dsm[:, 168:176], dsm[:, 24:32], dsm[:, 16:24], ALU.subtract).then_inc(decay_in, t.one("decay_in"))
            dve.wait_ge(decays, t.next("decays"))
            tt_(eD[:, :, :], eD[:, :, :], every(msk("strict")), ALU.mult).then_inc(dve_step, t.one("dve_step"))
            dve.wait_ge(dve_step, t.at("dve_step"))
            tt_(eD[:, :, :], eD[:, :, :], spread(dsm[:, 0:8]), ALU.mult).then_inc(dve_step, t.one("dve_step"))
            dve.wait_ge(dve_step, t.at("dve_step"))
            tt_(bR[:, :, :], bR[:, :, :], every(msk("strictT")), ALU.mult).then_inc(dve_step, t.one("dve_step"))
            dve.wait_ge(dve_step, t.at("dve_step"))
            tt_(bR[:, :, :], bR[:, :, :], eDT[:, :, :], ALU.mult).then_inc(dve_step, t.one("dve_step"))
            dve.wait_ge(dve_step, t.at("dve_step"))
            tt_(eDT[:, :, :], eDT[:, :, :], every(msk("tri")), ALU.mult).then_inc(dve_step, t.one("dve_step"))
            dve.wait_ge(dve_step, t.at("dve_step"))
            tt_(dsm[:, 176:184], dsm[:, 176:184], dsm[:, 0:8], ALU.mult).then_inc(dve_step, t.one("dve_step"))
            dve.wait_ge(dve_step, t.at("dve_step"))
            tt_(kb[:, :, :], ktok[:, :, :], spread(dsm[:, 176:184]), ALU.mult).then_inc(dve_step, t.one("dve_step"))
            dve.wait_ge(dve_step, t.at("dve_step"))
            tt_(ktail[:, :, :], ktok[:, :, :], spread(dsm[:, 184:192]), ALU.mult).then_inc(dve_step, t.one("dve_step"))
            dve.wait_ge(dve_step, t.at("dve_step"))
            for tt in range(2):
                dve.wait_ge(grams, t.next("grams"))
                b, r = quad(d_result()), slice(4 * tt, 4 * tt + 4)
                tt_(am[:, r, :], b, eD[:, r, :], ALU.mult).then_inc(dve_step, t.one("dve_step"))
                dve.wait_ge(dve_step, t.at("dve_step"))
                tt_(amT[:, r, :], b, bR[:, r, :], ALU.mult).then_inc(d_free, 1)
            for tt in range(2):
                r = slice(4 * tt, 4 * tt + 4)
                dve.wait_ge(grams, t.next("grams"))
                b = d_result()
                stt(qkT[:, r, :], quad(b), P ** -0.5, eDT[:, r, :],
                                                 ALU.mult, ALU.mult).then_inc(d_free, 1)
            mine()
            for tt in range(2):
                q = cy[:, 0:4, tt * P:tt * P + P]
                stt(q, q, P ** -0.5, expG[:, 4 * tt:4 * tt + 4, :], ALU.mult, ALU.mult).then_inc(dve_step, t.one("dve_step"))
                dve.wait_ge(dve_step, t.at("dve_step"))
            level = lambda name, l: every(msk(name)[:, l * P:l * P + P])
            tt_(tI[:, :, :], am[:, :, :], level("level", 0), ALU.mult).then_inc(dve_step, t.one("dve_step"))
            dve.wait_ge(dve_step, t.at("dve_step"))
            tt_(tI[:, :, :], every(ident), tI[:, :, :], ALU.subtract).then_inc(dve_step, t.one("dve_step"))
            dve.wait_ge(dve_step, t.at("dve_step"))
            tt_(tIT[:, :, :], amT[:, :, :], level("levelT", 0), ALU.mult).then_inc(dve_step, t.one("dve_step"))
            dve.wait_ge(dve_step, t.at("dve_step"))
            tt_(tIT[:, :, :], every(ident), tIT[:, :, :], ALU.subtract).then_inc(dve_step, t.one("dve_step"))
            dve.wait_ge(dve_step, t.at("dve_step"))
            for l in range(1, LEVELS):
                tt_(mL[:, :, :], amT[:, :, :], level("levelT", l), ALU.mult).then_inc(level_ready, t.one("level_ready"))
                for tt in range(2):
                    dve.wait_ge(inv, t.next("inv"))
                    b = d_result()
                    dve.tensor_copy(ut[:, 4 * tt:4 * tt + 4, :], quad(b)).then_inc(d_free, 1)
                for to in (tI, tIT):
                    for tt in range(2):
                        r = slice(4 * tt, 4 * tt + 4)
                        dve.wait_ge(inv, t.next("inv"))
                        b = d_result()
                        tt_(to[:, r, :], to[:, r, :], quad(b), ALU.subtract).then_inc(d_free, 1)
                mine()
            dve.memset(state[:, :, :], 0.0).then_inc(inv_ready, t.one("inv_ready"))
            dve.memset(vnew[:, :, :, :], 0.0).then_inc(state_ready, t.one("state_ready"))
            for to in (uu, wT):
                for tt in range(2):
                    dve.wait_ge(uw, t.next("uw"))
                    b = d_result()
                    dve.tensor_copy(to[:, 4 * tt:4 * tt + 4, :], quad(b)).then_inc(d_free, 1)
            mine()
            for c in range(SEQ // B_CHUNK):
                tt, half = c // 2, c % 2
                r = slice(64 * half, 64 * half + 64)
                dve.wait_ge(ws, t.next("ws"))
                b = d_result()
                tt_(vnew[r, tt, :, :], uu[r, 4 * tt:4 * tt + 4, :], quad(b)[r],
                                              ALU.subtract).then_inc(d_free, 1)
                dve.wait_ge(outs, t.next("outs"))
                b = d_result()
                dve.tensor_copy(oB[r, tt, :], b[r, :]).then_inc(d_free, 1)
                if c + 1 < SEQ // B_CHUNK:
                    dve.wait_ge(supd, t.next("supd"))
                    b = d_result()
                    for h in range(B_HEADS):
                        last = stt(state[:, h, :], state[:, h, :],
                                   expG[:, 4 * tt + h, 64 * half + 63:64 * half + 64],
                                   b[:, h * P:h * P + P], ALU.mult, ALU.add)
                    last.then_inc(d_free, 1)
                    mine()
            mine()
            ob = oB[:, :, :].rearrange("p t (h n) -> p (t h) n", n=P)
            oq = osq[:, :, :].rearrange("p t (h n) -> p (t h) n", n=P)
            tt_(oq, ob, ob, ALU.mult).then_inc(dve_step, t.one("dve_step"))
            dve.wait_ge(dve_step, t.at("dve_step"))
            dve.tensor_reduce(dsm[:, 192:200], oq, AX.X, ALU.add).then_inc(ob_ssq, t.one("ob_ssq"))
            dve.wait_ge(ob_root, t.next("ob_root"))
            recip(dsm[:, 200:208])
            tt_(ob, ob, spread(dsm[:, 200:208]), ALU.mult).then_inc(dve_step, t.one("dve_step"))
            dve.wait_ge(dve_step, t.at("dve_step"))
            tt_(ob, ob, every(row("hyb_norm_w")), ALU.mult).then_inc(dve_step, t.one("dve_step"))
            dve.wait_ge(dve_step, t.at("dve_step"))
            tt_(oB[:, :, :], oB[:, :, :], zt[:, :, :], ALU.mult).then_inc(mixed, t.one("mixed"))
            for k in range(KT):
                dve.wait_ge(turned, t.next("turned"))
                b = d_result()
                dve.tensor_copy(gH[:, k, :], b[:, 0:SEQ]).then_inc(dve_step, t.one("dve_step"))
                dve.wait_ge(dve_step, t.at("dve_step"))
                tt_(gL[:, k, :], b[:, 0:SEQ], gH[:, k, :].bitcast(F32), ALU.subtract).then_inc(d_free, 1)
            for c in range(4):
                chunk(2, lambda m, b: add_scaled(2 * c + m, b))
            layer_norm(0, "ln1_g", "ln1_b")
            mlp2(0)
            split_x()
            ts(small[:, 48:56], col("rec_lambda"), -1.0, None, ALU.mult).then_inc(dve_step, t.one("dve_step"))
            dve.wait_ge(dve_step, t.at("dve_step"))
            ts(small[:, 32:40], small[:, 48:56], 0.0, None, ALU.max).then_inc(dve_step, t.one("dve_step"))
            dve.wait_ge(dve_step, t.at("dve_step"))
            tt_(small[:, 48:56], small[:, 48:56], col("rec_lambda"), ALU.max).then_inc(soft_in, t.one("soft_in"))
            dve.memset(xr[:, :, 0:B_CONV - 1], 0.0).then_inc(dve_step, t.one("dve_step"))
            dve.wait_ge(dve_step, t.at("dve_step"))
            for c in range(4):
                chunk(2, lambda m, b: dve.tensor_copy(xr[:, 2 * c + m, B_CONV - 1:], b[:, 0:SEQ]))
            mine()
            causal(xr, xc, KT, "rec_conv", "rec_conv_b", "xc_ready")
            for k in range(KT):
                split_lo(xcL[:, k, :], xc[:, k, :], xcH[:, k, :], "xc_hi", "xc_split")
            dve.wait_ge(soft_exp, t.next("soft_exp"))
            log1p_exp(small[:, 56:64], small[:, 0:8], small[:, 8:16], small[:, 16:24], small[:, 32:40],
                      small[:, 24:32])
            ts(small[:, 40:48], small[:, 24:32], -LRU_C, None, ALU.mult).then_inc(c8_ready, t.one("c8_ready"))
            chunk(8)
            chunk(8)
            for c in range(4):
                chunk(2, lambda m, b: dve.tensor_copy(gg[:, 2 * c + m, :], b[:, 0:SEQ]))
            mine()
            dve.memset(small[:, 0:1], 0.0).then_inc(gg_in, t.one("gg_in"))
            dve.wait_ge(tanh_ready, t.next("tanh_ready", KT))
            dve.wait_ge(a_ready, t.next("a_ready", KT))
            tt_(gi[:, :, :], gi[:, :, :], xc[:, :, :], ALU.mult).then_inc(dve_step, t.one("dve_step"))
            dve.wait_ge(dve_step, t.at("dve_step"))
            tt_(xc[:, :, :], g3[:, :, :], g3[:, :, :], ALU.mult).then_inc(dve_step, t.one("dve_step"))
            dve.wait_ge(dve_step, t.at("dve_step"))
            for k in range(KT):
                stt(gt[:, k, :], xc[:, k, :], 1.0, gt[:, k, :], ALU.add, ALU.mult).then_inc(var_ready, t.one("var_ready"))
            for k in range(KT):
                dve.wait_ge(sqrt_ready, t.next("sqrt_ready"))
                tt_(gi[:, k, :], gi[:, k, :], gt[:, k, :], ALU.mult).then_inc(dve_step, t.one("dve_step"))
                dve.wait_ge(dve_step, t.at("dve_step"))
                dve.tensor_tensor_scan(xc[:, k, :], g3[:, k, :], gi[:, k, :], 0.0, ALU.mult, ALU.add).then_inc(dve_step, t.one("dve_step"))
                dve.wait_ge(dve_step, t.at("dve_step"))
            for k in range(KT):
                dve.wait_ge(gelu_ready, t.next("gelu_ready"))
                tt_(xc[:, k, :], xc[:, k, :], gg[:, k, :], ALU.mult).then_inc(hg_ready, t.one("hg_ready"))
            for k in range(KT):
                split_lo(xcL[:, k, :], xc[:, k, :], xcH[:, k, :], "xc_hi", "o_split")
            for c in range(4):
                chunk(2, lambda m, b: add_scaled(2 * c + m, b))
            layer_norm(1, "ln1_g", "ln1_b")
            mlp2(1)
            for g in range(4):
                dve.wait_ge(turned, t.next("turned"))
                dve.tensor_copy(outrow[:, g // 2, 512 * (g % 2):512 * (g % 2) + 512], d_result()).then_inc(out_ready, t.one("out_ready"))

        @block.gpsimd
        def _(pool):
            t = Tally(pool)

            def end_stage():
                pool.drain().then_inc(stage_pool, t.one("stage"))
                pool.wait_ge(stage_pe, t.at("stage"))
                pool.wait_ge(stage_act, t.at("stage"))
                pool.wait_ge(stage_dve, t.at("stage"))

            tt_ = pool.tensor_tensor

            def mlp(T):
                def squared(par):
                    for m in range(2):
                        pool.wait_ge(a_free, t.at("a", 1))
                        if not (t.j is None and t.n.get("ff", 0) < 4):
                            pool.wait_ge(ff_ready, t.at("ff", -3))
                        x = ff[:, m, 0:T]
                        tt_(ffsq[:, par, m, 0:T], x, x, ALU.mult).then_inc(ff_squared, 1)
                        t.up("a")
                        t.up("ff")

                squared(0)
                squared(1)
                with t.loop(FF_STEPS // 2 - 1, a=4, ff=4):
                    squared(0)
                    squared(1)

            def rotate(dst, tmp, src, cos, sin, half):
                tt_(tmp[0], src[1], sin[0], ALU.mult).then_inc(pool_step, t.one("pool_step"))
                tt_(tmp[1], src[0], sin[1], ALU.mult).then_inc(pool_step, t.one("pool_step"))
                tt_(dst[0], src[0], cos[0], ALU.mult).then_inc(pool_step, t.one("pool_step"))
                tt_(dst[1], src[1], cos[1], ALU.mult).then_inc(pool_step, t.one("pool_step"))
                pool.wait_ge(pool_step, t.at("pool_step"))

            pool.wait_ge(x_loaded, 16)
            pool.wait_ge(loaded, 48)
            pool.memset(small[:, 62:63], 0.0).then_inc(x_in, t.one("x_in"))
            end_stage()
            for l, segs in LAYERS:
                TX = segs * SEQ
                if l == 0:
                    end_stage()
                end_stage()
                t.up("a", 4)
                end_stage()
                for c in range(8):
                    n = (2 * segs if c < 4 else 4)
                    g = row("q_norm_g" if c < 4 else "k_norm_g", l * QK, QK)
                    pool.wait_ge(qk_normed, t.next("qk_normed"))
                    q = qs[:, c % 2, 0:n, :].rearrange("p t (g d) -> p (t g) d", d=QK)
                    tt_(q, q, g.unsqueeze(1).to_broadcast([P, 4 * n, QK]), ALU.mult).then_inc(pool_step, t.one("pool_step"))
                    pool.wait_ge(pool_step, t.at("pool_step"))
                    for tt in range(2):
                        x = qs[:, c % 2, tt, :].rearrange("p (g s d) -> p g s d", g=4, s=2)
                        m = qtmp[:, tt, :].rearrange("p (g s d) -> p g s d", g=4, s=2)
                        cs, sn = (con(w)[:, tt * QK:tt * QK + QK].rearrange("p (s d) -> p s d", s=2)
                                  for w in ("cos", "sin"))
                        wide = lambda v: v.unsqueeze(1).to_broadcast([P, 4, QK // 2])
                        for s in range(2):
                            tt_(m[:, :, s, :], x[:, :, 1 - s, :], wide(sn[:, s, :]), ALU.mult).then_inc(pool_step, t.one("pool_step"))
                        pool.wait_ge(pool_step, t.at("pool_step"))
                        for s in range(2):
                            tt_(x[:, :, s, :], x[:, :, s, :], wide(cs[:, s, :]), ALU.mult).then_inc(pool_step, t.one("pool_step"))
                    pool.wait_ge(pool_step, t.at("pool_step"))
                    tt_(qs[:, c % 2, 0:2, :], qs[:, c % 2, 0:2, :], qtmp[:, :, :], ALU.add).then_inc(qk_ready, t.one("qk_ready"))
                    pool.wait_ge(qk_ready, t.at("qk_ready"))
                t.n["chunk"] = CHUNK_OF_VALUES[l]
                for _ in range(4):
                    s = t.slot("chunk", RAW, AHEAD)
                    pool.wait_ge(hi_done, t.at("chunk", AHEAD + 1))
                    tt_(w_lo[:, s, :], raw[:, s, :], w_hi[:, s, :].bitcast(F32), ALU.subtract).then_inc(lo_done, 1)
                    t.up("chunk")
                t.up("a", 16 + 16)
                end_stage()
                t.n["chunk"] = CHUNK_OF_FILLS[l]
                for _ in fills_of(l):
                    s = t.slot("chunk", RAW, AHEAD)
                    pool.wait_ge(hi_done, t.at("chunk", AHEAD + 1))
                    tt_(w_lo[:, s, :], raw[:, s, :], w_hi[:, s, :].bitcast(F32), ALU.subtract).then_inc(lo_done, 1)
                    t.up("chunk")
                end_stage()
                t.up("a", 8 + 8)
                end_stage()
                mlp(TX)
                end_stage()

            pool.dma_start(masks[:, :], a["masks"]).then_inc(masks_loaded, 16)
            pool.dma_start(w8[:, :, :], a["w_tail"]).then_inc(masks_loaded, 16)
            pool.wait_ge(qa_in, t.next("qa_in"))
            for tt in range(2):
                cs, sn = (con(w)[:, tt * A_DH:tt * A_DH + A_DH].rearrange("p (s d) -> p s d", s=2)
                          for w in ("cos2", "sin2"))
                xq = qa[:, tt, 0:512].rearrange("p (v a s d) -> p v a s d", v=2, a=4, s=2)
                yq = qr[:, tt, 0:512].rearrange("p (a v s d) -> p v a s d", v=2, a=4, s=2)
                mq = qtmp2[:, tt, 0:512].rearrange("p (a v s d) -> p v a s d", v=2, a=4, s=2)
                xk = qa[:, tt, 512:640].rearrange("p (v s d) -> p v s d", v=2, s=2)
                yk = qr[:, tt, 512:640].rearrange("p (v s d) -> p v s d", v=2, s=2)
                mk = qtmp2[:, tt, 512:640].rearrange("p (v s d) -> p v s d", v=2, s=2)
                for s in range(2):
                    for kv in range(A_KV):
                        w4 = lambda v: v.unsqueeze(1).to_broadcast([P, 4, A_DH // 2])
                        tt_(mq[:, kv, :, s, :], xq[:, kv, :, 1 - s, :], w4(sn[:, s, :]), ALU.mult)
                        tt_(yq[:, kv, :, s, :], xq[:, kv, :, s, :], w4(cs[:, s, :]), ALU.mult)
                    w2 = lambda v: v.unsqueeze(1).to_broadcast([P, 2, A_DH // 2])
                    tt_(mk[:, :, s, :], xk[:, :, 1 - s, :], w2(sn[:, s, :]), ALU.mult)
                    tt_(yk[:, :, s, :], xk[:, :, s, :], w2(cs[:, s, :]), ALU.mult).then_inc(pool_step, t.one("pool_step"))
                    pool.wait_ge(pool_step, t.at("pool_step"))
            pool.wait_ge(masks_loaded, 32)
            pool.memset(small[:, 63:64], 0.0).then_inc(masks_in, t.one("masks_in"))
            tt_(qr[:, :, :], qr[:, :, :], qtmp2[:, :, :], ALU.add).then_inc(qa_ready, t.one("qa_ready"))
            pool.wait_ge(qa_ready, t.at("qa_ready"))
            t.up("a", 4 + 5 + 8)
            end_stage()
            end_stage()
            mlp(SEQ)
            end_stage()
            t.up("a", 16)
            end_stage()
            mlp(SEQ)
            end_stage()


def pack(table, n, parts):
    out = np.zeros((P, n), np.float32)
    for name, (at, w) in table.items():
        out[:, at:at + w] = parts[name]
    return out


def by_column(v):
    v = np.asarray(v)
    return np.moveaxis(v.reshape(-1, P), 1, 0)


def taps(w):
    w = np.asarray(w)
    n, k, c = w.shape
    return w.reshape(n, k, c // P, P).transpose(3, 0, 2, 1).reshape(P, -1)


def kernel(**inputs):
    import concourse.bacc as bacc
    from concourse.bass_utils import run_bass_kernel_spmd

    x = {k: np.asarray(v) for k, v in inputs.items()}
    cols = pack(COLS, COLS_N, {
        "cond": np.stack([by_column(x["c"]), by_column(x["c_ctx"])], 2).reshape(P, -1),
        "b_ada": by_column(x["b_ada"]), "norm1_g": by_column(x["norm1_g"]), "norm2_g": by_column(x["norm2_g"]),
        "b_gate": by_column(x["b_gate"]), "w_dw": taps(x["w_dw"]), "b_dw": by_column(x["b_dw"]),
        "conv_ln_g": by_column(x["conv_ln_g"]), "conv_ln_b": by_column(x["conv_ln_b"]),
        "hyb_conv": taps(x["hyb_conv_w_2"]), "rec_conv": taps(x["rec_conv_w_2"]),
        "rec_conv_b": by_column(x["rec_conv_b_2"]), "rec_b_a": by_column(x["rec_b_a_2"]),
        "rec_b_x": by_column(x["rec_b_x_2"]), "rec_lambda": by_column(x["rec_lambda_2"]),
        "ln1_g": by_column(x["ln1_g_2"]), "ln1_b": by_column(x["ln1_b_2"]),
        "ln2_g": by_column(x["ln2_g_2"]), "ln2_b": by_column(x["ln2_b_2"])})
    rows = pack(ROWS, ROWS_N, {
        "q_norm_g": x["q_norm_g"].reshape(1, -1), "k_norm_g": x["k_norm_g"].reshape(1, -1),
        "attn_norm_g": x["attn_norm_g"].reshape(1, -1), "lam_q": x["lam_q"].reshape(1, -1),
        "lam_k": x["lam_k"].reshape(1, -1),
        "sinks": x["hyb_sinks_2"].reshape(A_KV, A_HEADS // A_KV).T.reshape(1, -1),
        "a_log": x["hyb_a_log_2"].reshape(1, -1), "dt_bias": x["hyb_dt_bias_2"].reshape(1, -1),
        "hyb_norm_w": x["hyb_norm_w_2"].reshape(1, -1)})
    consts, masks = shape_constants()
    weights = np.empty((CHUNKS, P, CHUNK), np.float32)
    for n, (name, l, kts, c) in enumerate(chunk_plan()):
        w = x[name][l]
        if kts is None:
            weights[n] = w.reshape(LRU_BLOCKS * 2, P, CC).transpose(1, 0, 2).reshape(P, CHUNK)
        else:
            part = w[kts.start * P:kts.stop * P, c.start:c.stop]
            weights[n] = part.reshape(len(kts), P, len(c)).transpose(1, 0, 2).reshape(P, CHUNK)
    arrays = {
        "x_rows": np.concatenate([x["x"][0], x["ctx"][0]]).reshape(4, P, D).transpose(1, 0, 2).copy(),
        "cols": cols, "rows": rows, "consts": consts, "masks": masks, "weights": weights,
        "w_tail": x["hyb_w_in_2"][0][:, -HYB_TAIL:].reshape(KT, P, HYB_TAIL).transpose(1, 0, 2).copy()}
    nc = bacc.Bacc("TRN2", target_bir_lowering=False, num_devices=1)
    aps = {k: nc.dram_tensor(f"in_{k}", v.shape, F32, kind="ExternalInput").ap() for k, v in arrays.items()}
    out = nc.dram_tensor("out_0", (1, SEQ, D), F32, kind="ExternalOutput").ap()
    aps["out"] = out.rearrange("b (t p) d -> p (b t) d", p=P)
    build_program(nc, aps)
    r = run_bass_kernel_spmd(nc, [{f"in_{k}": v for k, v in arrays.items()}], core_ids=[0])
    return r.results[0]["out_0"]
```
